# Optimizing a Trainium2 kernel written in Bass

```python
import math
import jax, jax.numpy as jnp
from jax import lax
import numpy as np

D_MODEL = 2048
BATCH = 1
SEQ = 256
DEPTH = 2

N_EVEN = (DEPTH + 1) // 2
N_ODD = DEPTH // 2

DIFF_HEADS = 8
DIFF_QK_DIM = 64
DIFF_V_DIM = 2 * DIFF_QK_DIM
DIFF_WIDTH = DIFF_HEADS * DIFF_V_DIM
ROT_DIM = DIFF_QK_DIM // 4
ROPE_THETA = 500000.0
Q_BLOCK = 128

HG_HEADS = 8
HG_HEAD_DIM = 128
HG_WIDTH = HG_HEADS * HG_HEAD_DIM
HG_CHUNK = 64

EVEN_SPLIT_SIZES = [DIFF_WIDTH] * 3 + [HG_WIDTH] * 5
EVEN_IN_WIDTH = sum(EVEN_SPLIT_SIZES)
EVEN_SPLITS = [int(s) for s in np.cumsum(EVEN_SPLIT_SIZES)[:-1]]
EVEN_OUT_WIDTH = DIFF_WIDTH + HG_WIDTH

S5_GROUP = 16
S5_GROUPS = D_MODEL // S5_GROUP
S5_STATE = 64
S5_GROUPS_PER_BLOCK = 8

D_FF = 4 * D_MODEL

ALPHA = (2 * DEPTH) ** 0.25
BETA = (8 * DEPTH) ** -0.25
LN_EPS = 1e-5
RMS_EPS = 1e-6

kernel_name = 'hybrid_diffattn_hgrn2_s5_deepnorm_adaln'

def layer_norm(x, g, b):
    xf = x.astype(jnp.float32)
    mu = jnp.mean(xf, axis=-1, keepdims=True)
    var = jnp.mean(jnp.square(xf - mu), axis=-1, keepdims=True)
    return ((xf - mu) * lax.rsqrt(var + LN_EPS)).astype(x.dtype) * g + b

def rms_norm(x, g):
    xf = x.astype(jnp.float32)
    return (xf * lax.rsqrt(jnp.mean(xf * xf, axis=-1, keepdims=True) + RMS_EPS)).astype(x.dtype) * g

def adaln(c_act, w, b):
    m = c_act @ w + b
    shift, scale, gate = jnp.split(m, 3, axis=-1)
    return shift[:, None, :], scale[:, None, :], gate[:, None, :]

def rotary_tables(seq_len):
    pos = jnp.arange(seq_len, dtype=jnp.float32)
    inv_freq = 1.0 / (ROPE_THETA ** (jnp.arange(0, ROT_DIM, 2, dtype=jnp.float32) / ROT_DIM))
    ang = pos[:, None] * inv_freq[None, :]
    return jnp.cos(ang), jnp.sin(ang)

def partial_rotary(t, cos, sin):
    half = ROT_DIM // 2
    cos = cos[None, :, None, None, :]
    sin = sin[None, :, None, None, :]
    tf = t.astype(jnp.float32)
    x1, x2 = tf[..., :half], tf[..., half:ROT_DIM]
    out = jnp.concatenate([x1 * cos - x2 * sin, x2 * cos + x1 * sin, tf[..., ROT_DIM:]], axis=-1)
    return out.astype(t.dtype)

def diff_attention(q, k, v, lam):
    B, L, H, _, dqk = q.shape
    nb = L // Q_BLOCK
    scale = dqk ** -0.5
    qb = q.reshape(B, nb, Q_BLOCK, H, 2, dqk).transpose(1, 0, 2, 3, 4, 5)

    def one_block(q_blk):
        s = jnp.einsum('bqhcd,bkhcd->bhcqk', q_blk, k).astype(jnp.float32) * scale
        p = jax.nn.softmax(s, axis=-1)
        a = p[:, :, 0] - lam * p[:, :, 1]
        return jnp.einsum('bhqk,bkhe->bqhe', a.astype(v.dtype), v)

    o = lax.map(one_block, qb)
    return o.transpose(1, 0, 2, 3, 4).reshape(B, L, H, v.shape[-1])

def gla_chunk_scan(q, k, v, logf):
    B, L, H, dk = q.shape
    dv = v.shape[-1]
    n = L // HG_CHUNK

    def to_chunks(t):
        return t.reshape(B, n, HG_CHUNK, H, t.shape[-1]).transpose(1, 0, 3, 2, 4)

    lower = jnp.tril(jnp.ones((HG_CHUNK, HG_CHUNK), dtype=bool))[:, :, None]

    def step(S, inp):
        qc, kc, vc, gc = inp
        b = jnp.cumsum(gc, axis=2)
        o_inter = jnp.einsum('bhtd,bhde->bhte', qc * jnp.exp(b), S)
        rel = jnp.exp(jnp.where(lower, b[:, :, :, None, :] - b[:, :, None, :, :], -jnp.inf))
        scores = jnp.einsum('bhtd,bhtsd,bhsd->bhts', qc, rel, kc)
        o_intra = jnp.einsum('bhts,bhse->bhte', scores, vc)
        b_end = b[:, :, -1:, :]
        S_new = jnp.exp(b_end[:, :, 0, :, None]) * S + jnp.einsum('bhsd,bhse->bhde', kc * jnp.exp(b_end - b), vc)
        return S_new, o_inter + o_intra

    S0 = jnp.zeros((B, H, dk, dv), jnp.float32)
    _, o = lax.scan(step, S0, (to_chunks(q), to_chunks(k), to_chunks(v), to_chunks(logf)))
    return o.transpose(1, 0, 3, 2, 4).reshape(B, L, H, dv)

def hgrn2(q_raw, f_fwd_raw, f_bwd_raw, i_raw, g_raw, lb, norm_g):
    B, L, _ = q_raw.shape
    heads = lambda t: t.reshape(B, L, HG_HEADS, HG_HEAD_DIM)
    q = heads(jax.nn.silu(q_raw.astype(jnp.float32)))
    v = heads(i_raw.astype(jnp.float32))

    def direction(f_raw, lb_dir, reverse):
        f = lb_dir + (1.0 - lb_dir) * jax.nn.sigmoid(f_raw.astype(jnp.float32))
        k, logf = heads(1.0 - f), heads(jnp.log(f))
        if reverse:
            flip = lambda t: jnp.flip(t, axis=1)
            return flip(gla_chunk_scan(flip(q), flip(k), flip(v), flip(logf)))
        return gla_chunk_scan(q, k, v, logf)

    o = direction(f_fwd_raw, lb[0], False) + direction(f_bwd_raw, lb[1], True)
    o = rms_norm(o, norm_g) * jax.nn.silu(heads(g_raw))
    return o.astype(g_raw.dtype)

def even_mixer(h, w_in, w_out, diff_lambda, subln_g, lb, hg_norm_g, cos, sin, lam_init):
    B, L, _ = h.shape
    proj = h @ w_in
    qa, ka, va, qb, f_fwd, f_bwd, ib, gb = jnp.split(proj, EVEN_SPLITS, axis=-1)
    qa = partial_rotary(qa.reshape(B, L, DIFF_HEADS, 2, DIFF_QK_DIM), cos, sin)
    ka = partial_rotary(ka.reshape(B, L, DIFF_HEADS, 2, DIFF_QK_DIM), cos, sin)
    va = va.reshape(B, L, DIFF_HEADS, DIFF_V_DIM)
    lf = diff_lambda.astype(jnp.float32)
    lam = jnp.exp(jnp.sum(lf[0] * lf[1])) - jnp.exp(jnp.sum(lf[2] * lf[3])) + lam_init
    oa = rms_norm(diff_attention(qa, ka, va, lam), subln_g) * (1.0 - lam_init)
    ob = hgrn2(qb, f_fwd, f_bwd, ib, gb, lb, hg_norm_g)
    o = jnp.concatenate([oa.reshape(B, L, DIFF_WIDTH).astype(h.dtype), ob.reshape(B, L, HG_WIDTH)], axis=-1)
    return o @ w_out

def complex_affine_combine(e1, e2):
    a1r, a1i, x1r, x1i = e1
    a2r, a2i, x2r, x2i = e2
    return (a2r * a1r - a2i * a1i,
            a2r * a1i + a2i * a1r,
            a2r * x1r - a2i * x1i + x2r,
            a2r * x1i + a2i * x1r + x2i)

def s5_direction(u, lam_re, lam_im, log_dt, b_re, b_im, c_re, c_im, reverse):
    dt = jnp.exp(log_dt)[:, None]
    mag = jnp.exp(lam_re * dt)
    ab_re, ab_im = mag * jnp.cos(lam_im * dt), mag * jnp.sin(lam_im * dt)
    den = lam_re * lam_re + lam_im * lam_im
    coef_re = ((ab_re - 1.0) * lam_re + ab_im * lam_im) / den
    coef_im = (ab_im * lam_re - (ab_re - 1.0) * lam_im) / den
    bb_re = coef_re[..., None] * b_re - coef_im[..., None] * b_im
    bb_im = coef_re[..., None] * b_im + coef_im[..., None] * b_re
    bu_re = jnp.einsum('blgh,gph->blgp', u, bb_re)
    bu_im = jnp.einsum('blgh,gph->blgp', u, bb_im)
    a_re = jnp.broadcast_to(ab_re, bu_re.shape)
    a_im = jnp.broadcast_to(ab_im, bu_re.shape)
    _, _, s_re, s_im = lax.associative_scan(complex_affine_combine, (a_re, a_im, bu_re, bu_im),
                                            reverse=reverse, axis=1)
    return jnp.einsum('blgp,ghp->blgh', s_re, c_re) - jnp.einsum('blgp,ghp->blgh', s_im, c_im)

def s5_mixer(h, lam_re, lam_im, log_dt, b_re, b_im, c_re, c_im, d_skip, w_glu):
    B, L, D = h.shape
    nb = S5_GROUPS // S5_GROUPS_PER_BLOCK

    def group_blocks(p):
        p = p.astype(jnp.float32)
        return jnp.moveaxis(p.reshape(p.shape[0], nb, S5_GROUPS_PER_BLOCK, *p.shape[2:]), 1, 0)

    u = jnp.moveaxis(h.astype(jnp.float32).reshape(B, L, nb, S5_GROUPS_PER_BLOCK, S5_GROUP), 2, 0)
    d = d_skip.astype(jnp.float32).reshape(nb, S5_GROUPS_PER_BLOCK, S5_GROUP)

    def run_block(args):
        u_b, lre, lim, ldt, bre, bim, cre, cim, d_b = args
        y = d_b * u_b
        for dr in range(2):
            y = y + s5_direction(u_b, lre[dr], lim[dr], ldt[dr], bre[dr], bim[dr], cre[dr], cim[dr],
                                 reverse=(dr == 1))
        return y

    ys = lax.map(run_block, (u, group_blocks(lam_re), group_blocks(lam_im), group_blocks(log_dt),
                             group_blocks(b_re), group_blocks(b_im), group_blocks(c_re), group_blocks(c_im), d))
    y = jnp.moveaxis(ys, 0, 2).reshape(B, L, D)
    z = jax.nn.gelu(y).astype(h.dtype) @ w_glu
    a, g = jnp.split(z, 2, axis=-1)
    return a * jax.nn.sigmoid(g)

def squared_relu_mlp(h, w1, w2):
    return jnp.square(jax.nn.relu(h @ w1)) @ w2

def setup_inputs(seed: int = 0) -> dict:
    key = jax.random.key(seed)
    ks = jax.random.split(key, 24)
    f32 = jnp.float32
    nrm = lambda k, shape, s: jax.random.normal(k, shape, f32) * s
    n_state = jnp.arange(S5_STATE, dtype=f32)
    return {
        'x': nrm(ks[0], (BATCH, SEQ, D_MODEL), 1.0),
        'c': nrm(ks[1], (BATCH, D_MODEL), 1.0),
        'ada_w': nrm(ks[2], (DEPTH, 2, D_MODEL, 3 * D_MODEL), 0.5 * D_MODEL ** -0.5),
        'ada_b': nrm(ks[3], (DEPTH, 2, 3 * D_MODEL), 0.01),
        'ln_g': 1.0 + nrm(ks[4], (DEPTH, 2, D_MODEL), 0.02),
        'ln_b': nrm(ks[5], (DEPTH, 2, D_MODEL), 0.02),
        'mix_w_in': nrm(ks[6], (N_EVEN, D_MODEL, EVEN_IN_WIDTH), D_MODEL ** -0.5),
        'mix_w_out': nrm(ks[7], (N_EVEN, EVEN_OUT_WIDTH, D_MODEL), BETA * EVEN_OUT_WIDTH ** -0.5),
        'diff_lambda': nrm(ks[8], (N_EVEN, 4, DIFF_QK_DIM), 0.1),
        'diff_subln_g': 1.0 + nrm(ks[9], (N_EVEN, DIFF_V_DIM), 0.02),
        'hg_lower_bound': nrm(ks[10], (2, DEPTH + 1, HG_WIDTH), 0.1),
        'hg_norm_g': 1.0 + nrm(ks[11], (N_EVEN, HG_HEAD_DIM), 0.02),
        's5_lambda_re': -0.5 + nrm(ks[12], (N_ODD, 2, S5_GROUPS, S5_STATE), 0.01),
        's5_lambda_im': jnp.pi * n_state + nrm(ks[13], (N_ODD, 2, S5_GROUPS, S5_STATE), 0.01),
        's5_log_dt': jax.random.uniform(ks[14], (N_ODD, 2, S5_GROUPS), f32,
                                        minval=math.log(1e-3), maxval=math.log(1e-1)),
        's5_b_re': nrm(ks[15], (N_ODD, 2, S5_GROUPS, S5_STATE, S5_GROUP), (2 * S5_GROUP) ** -0.5),
        's5_b_im': nrm(ks[16], (N_ODD, 2, S5_GROUPS, S5_STATE, S5_GROUP), (2 * S5_GROUP) ** -0.5),
        's5_c_re': nrm(ks[17], (N_ODD, 2, S5_GROUPS, S5_GROUP, S5_STATE), S5_STATE ** -0.5),
        's5_c_im': nrm(ks[18], (N_ODD, 2, S5_GROUPS, S5_GROUP, S5_STATE), S5_STATE ** -0.5),
        's5_d': nrm(ks[19], (N_ODD, D_MODEL), 1.0),
        's5_w_glu': nrm(ks[20], (N_ODD, D_MODEL, 2 * D_MODEL), BETA * D_MODEL ** -0.5),
        'mlp_w1': nrm(ks[21], (DEPTH, D_MODEL, D_FF), D_MODEL ** -0.5),
        'mlp_w2': nrm(ks[22], (DEPTH, D_FF, D_MODEL), BETA * D_FF ** -0.5),
    }

def reference(x, c, ada_w, ada_b, ln_g, ln_b, mix_w_in, mix_w_out, diff_lambda, diff_subln_g,
              hg_lower_bound, hg_norm_g, s5_lambda_re, s5_lambda_im, s5_log_dt, s5_b_re, s5_b_im,
              s5_c_re, s5_c_im, s5_d, s5_w_glu, mlp_w1, mlp_w2):
    L = x.shape[1]
    cos, sin = rotary_tables(L)
    c_act = jax.nn.silu(c)
    lb_table = jnp.cumsum(jax.nn.softmax(hg_lower_bound.astype(jnp.float32), axis=1), axis=1)
    for layer in range(DEPTH):
        shift, scale, gate = adaln(c_act, ada_w[layer, 0], ada_b[layer, 0])
        h = x * (1.0 + scale) + shift
        if layer % 2 == 0:
            e = layer // 2
            lam_init = 0.8 - 0.6 * math.exp(-0.3 * layer)
            y = even_mixer(h, mix_w_in[e], mix_w_out[e], diff_lambda[e], diff_subln_g[e],
                           lb_table[:, layer], hg_norm_g[e], cos, sin, lam_init)
        else:
            o = layer // 2
            y = s5_mixer(h, s5_lambda_re[o], s5_lambda_im[o], s5_log_dt[o], s5_b_re[o], s5_b_im[o],
                         s5_c_re[o], s5_c_im[o], s5_d[o], s5_w_glu[o])
        x = layer_norm(ALPHA * x + (1.0 + gate) * y, ln_g[layer, 0], ln_b[layer, 0])
        shift, scale, gate = adaln(c_act, ada_w[layer, 1], ada_b[layer, 1])
        h = x * (1.0 + scale) + shift
        y = squared_relu_mlp(h, mlp_w1[layer], mlp_w2[layer])
        x = layer_norm(ALPHA * x + (1.0 + gate) * y, ln_g[layer, 1], ln_b[layer, 1])
    return x


_drawn_inputs = setup_inputs


def setup_inputs(seed=0):
    import zlib

    import numpy as np

    out = dict(_drawn_inputs(seed))
    spreads = {}
    factors = {'ada_b': 3.899,
     'diff_lambda': 3.786,
     'diff_subln_g': 27.623,
     'hg_lower_bound': 8.0,
     'hg_norm_g': 33.853,
     's5_lambda_re': 64.0,
     's5_lambda_im': 24.448,
     's5_log_dt': 29.936,
     's5_b_re': 33.824,
     's5_b_im': 33.896,
     's5_c_re': 33.784,
     's5_c_im': 34.632}
    for name, (base, spread) in spreads.items():
        noise = np.random.default_rng([zlib.crc32(name.encode()), seed]).standard_normal(out[name].shape)
        drawn = base * np.exp(spread * noise) if base else spread * noise
        out[name] = __import__('jax').numpy.asarray(drawn.astype(out[name].dtype))
    for name, factor in factors.items():
        out[name] = (out[name] * factor).astype(out[name].dtype)
    return out
```

```python
import math

import numpy as np
import concourse.bass as bass
from concourse import mybir

F = mybir.dt.float32
R = mybir.dt.float32r
I32 = mybir.dt.int32
ALU = mybir.AluOpType
ACT = mybir.ActivationFunctionType
AX = mybir.AxisListType

P = 128
D = 2048
T = 256
KT = D // P
DFF = 4 * D
HEADS = 8
LEVELS = 8
SLAB = 2048
ALPHA = 4 ** 0.25
LN_EPS, RMS_EPS = 1e-5, 1e-6
LAM_INIT = 0.8 - 0.6 * math.exp(0.0)
QK_SCALE = 64 ** -0.5
C4 = 4
NCH = T // C4
TILES5 = 64
MAGIC = 1.5 * 2 ** 23
ADA_HALF = 1024
ADA_COLS = 3072
GELU_C = math.sqrt(2 / math.pi)
PRIME_RAW, PRIME_USED, PRIME_EVAC, PRIME_ADA, PRIME_MAT = 4, 2, 2, 3, 1


def trunk(nc, a, out):
    sems = {}

    def S(name):
        if name not in sems:
            sems[name] = nc.alloc_semaphore(name)
        return sems[name]

    X = nc.alloc_sbuf_tensor("X", [P, KT, T], F)
    h_base = nc.sbuf_base
    Hhi = nc.alloc_sbuf_tensor("Hhi", [P, KT, T], R)
    Hlo = nc.alloc_sbuf_tensor("Hlo", [P, KT, T], R)
    HF = nc.alloc_sbuf_tensor_at("HF", [P, 8192], F, offset=h_base)
    Pb = nc.alloc_sbuf_tensor("Pb", [P, 64, T], F)
    PF = Pb[:].rearrange("p a t -> p (a t)")
    raw = nc.alloc_sbuf_tensor("raw", [P, 4, SLAB], F)
    w_base = nc.sbuf_base
    whi = nc.alloc_sbuf_tensor("whi", [P, 2, SLAB], R)
    wlo = nc.alloc_sbuf_tensor("wlo", [P, 2, SLAB], R)
    WF = nc.alloc_sbuf_tensor_at("WF", [P, 8192], F, offset=w_base)
    acc = nc.alloc_sbuf_tensor("acc", [P, ADA_COLS], F)
    araw = nc.alloc_sbuf_tensor("araw", [P, 3, ADA_HALF], F)
    ident = nc.alloc_sbuf_tensor("ident", [P, P], F)
    ones = nc.alloc_sbuf_tensor("ones", [P, T], F)
    PT = nc.alloc_sbuf_tensor("PT", [P, 4, P], F)
    MOD = nc.alloc_sbuf_tensor("MOD", [P, 4, 48], F)
    HA = nc.alloc_sbuf_tensor("HA", [P, 2, KT], F)
    G1 = nc.alloc_sbuf_tensor("G1", [P, 4, KT], F)
    cact = nc.alloc_sbuf_tensor("cact", [P, KT], F)
    small = nc.alloc_sbuf_tensor("small", [P, 64], F)
    lbs = nc.alloc_sbuf_tensor("lbs", [P, 2, 16], F)
    lamb = nc.alloc_sbuf_tensor("lamb", [P, 2], F)
    eps = nc.alloc_sbuf_tensor("eps", [P, 2], F)
    A4 = nc.alloc_sbuf_tensor("A4", [P, 4, P], F)
    Dsk = nc.alloc_sbuf_tensor("Dsk", [P, TILES5], F)
    PS = nc.alloc_psum_tensor("PS", [P, 8, 512], F)
    vmat = nc.dram_tensor("vmat", [16, P, SLAB], F, kind="Internal").ap()
    omat = nc.dram_tensor("omat", [20, P, SLAB], F, kind="Internal").ap()

    ADAB = [PT[:, i // 2, 48 * (i % 2):48 * (i % 2) + 48] for i in range(4)]
    LNG = [PT[:, 2, 16 * i:16 * i + 16] for i in range(4)]
    LNB = [PT[:, 2, 64 + 16 * i:80 + 16 * i] for i in range(4)]
    CRAW, LBR = PT[:, 3, 0:16], PT[:, 3, 16:64]
    SUBG, HGG = PT[:, 3, 64:65], PT[:, 3, 65:66]

    def bank(b, n=1):
        return PS[:, b:b + n, :].rearrange("p b c -> p (b c)")

    def settle(eng):
        eng.sem_inc(S("settled"), 1)

    def chain(eng, name):
        count = [0]

        def link(ins):
            count[0] += 1
            ins.then_inc(S(name), 1)
            eng.wait_ge(S(name), count[0])
        return link

    STG = WF[:, 0:512].rearrange("p (a c) -> p a c", a=4)
    LS = WF[:, 512:1280].rearrange("p (a c) -> p a c", a=6)
    LDT = WF[:, 1280:1284].rearrange("p (a c) -> p a c", a=2)
    DST = WF[:, 1536:1664].rearrange("p (a c) -> p a c", a=4)
    LAMR = WF[:, 1664:1920].rearrange("p (a c) -> p a c", a=4)
    LTMP = WF[:, 1920:2048].rearrange("p (a c) -> p a c", a=2)
    VS = WF[:, 2048:4096].rearrange("p (d c t m) -> p d c t m", d=2, c=2, t=4)
    Op = WF[:, 4096:6656].rearrange("p (c t s m) -> p c t s m", c=2, t=8, s=5)
    TP = WF[:, 6656:7936].rearrange("p (a x) -> p a x", a=2)
    Vp = PF[:, 4096:6144].rearrange("p (c t s m) -> p c t s m", c=2, t=8, s=4)
    INTRA = PF[:, 0:2048].rearrange("p (t m) -> p t m", t=16)
    TG = PF[:, 2048:3328].rearrange("p (a x) -> p a x", a=2)
    Bn = PF[:, 6144:10240].rearrange("p (c x h) -> p c x h", c=2, h=16)
    Cn = PF[:, 10240:14336].rearrange("p (a t x) -> p a t x", a=4, t=8)
    CTt = HF[:, 0:4096].rearrange("p (c x h) -> p c x h", c=2, h=16)
    BB = HF[:, 4096:8192].rearrange("p (c x h) -> p c x h", c=2, h=16)
    PW = PF[:, 14336:15360].rearrange("p (k c x) -> p k c x", k=4, c=2)
    TM = PF[:, 15360:16384].rearrange("p (a x) -> p a x", a=8)
    PWV = PF[:, 10240:11264].rearrange("p (c x s) -> p c x s", c=2, s=4)
    PWO = PF[:, 11264:13184].rearrange("p (c x s) -> p c x s", c=3, s=5)
    XN = PF[:, 0:4096].rearrange("p (a d) -> p a d", a=2)

    ada_w = a["ada_w"].rearrange("l s k m -> (l s k) m")

    def ada_loads(sp, i, q0, sub, c):
        for r in range(6):
            sp.wait_ge(S("ada_used"), i * 6 + (q0 + r + 1))
            row = (i * 2 + (sub * KT + r // 3)) * P
            sp.dma_start(araw[:, r % 3, :],
                         ada_w[bass.ds(row, P), c * ADA_COLS + (r % 3) * ADA_HALF:
                               c * ADA_COLS + (r % 3 + 1) * ADA_HALF]).then_inc(S(f"ada_ready{r % 3}"), 16)

    def ada_mac(v, i, q0, r):
        v.wait_ge(S(f"ada_ready{r % 3}"), (i * 2 + (q0 // 3 + r // 3 + 1)) * 16)
        v.wait_ge(S("ada_used"), i * 6 + (q0 + r + 1))
        cols = acc[:, (r % 3) * ADA_HALF:(r % 3 + 1) * ADA_HALF]
        nc.vector.scalar_tensor_tensor(out=cols, in0=araw[:, r % 3, :],
                                       scalar=cact[:, bass.ds(i * 2 + r // 3, 1)], in1=cols,
                                       op0=ALU.mult, op1=ALU.add).then_inc(S("ada_used"), 1)

    def ada_sum_pe(pe, n, q_end, b):
        pe.wait_ge(S("ada_used"), q_end + PRIME_ADA)
        for m in range(24):
            last = nc.tensor.matmul(PS[:, b, m:m + 1], acc[:, m * P:(m + 1) * P], ones[:, 0:1],
                                    start=True, stop=True)
        last.then_inc(S("ada_summed"), 1)

    def ada_finish(v, link, n, sub, c, b):
        v.wait_ge(S("ada_summed"), n + 1)
        link(nc.vector.tensor_tensor(MOD[:, sub, 24 * c:24 * c + 24], PS[:, b, 0:24],
                                     ADAB[sub][:, 24 * c:24 * c + 24], ALU.add))
        link(nc.vector.memset(acc[:], 0.0))
        v.sem_inc(S("ada_freed"), 1)

    def slab_loads(sp, i, B, G, src):
        for s in range(4):
            sp.wait_ge(S("lo_done"), i * 4 + (G + s + 1))
            sp.dma_start(raw[:, s, :], src(i, s)).then_inc(S(f"raw_ready{s}"), 16)

    def split_hi(act, i, B, G, s):
        act.wait_ge(S(f"raw_ready{s}"), i * 16 + (B + 1) * 16)
        act.wait_ge(S("slab_used"), i * 4 + (G + s + 1))
        nc.scalar.activation(whi[:, s % 2, :], raw[:, s, :], ACT.Copy).then_inc(S("hi_done"), 1)

    def split_lo(v, i, B, G, s):
        v.wait_ge(S("hi_done"), i * 4 + (G + s + 1))
        nc.vector.tensor_tensor(wlo[:, s % 2, :], raw[:, s, :], whi[:, s % 2, :].bitcast(F),
                                ALU.subtract).then_inc(S("lo_done"), 1)

    def three(ps, w, xh, xl, first, last):
        nc.tensor.matmul(ps, w[0], xh, start=first, stop=False, skip_group_check=True)
        nc.tensor.matmul(ps, w[0], xl, start=False, stop=False, skip_group_check=True)
        return nc.tensor.matmul(ps, w[1], xh, start=False, stop=last, skip_group_check=True)

    def block_products(pe, evacs, slabs, par):
        pe.wait_ge(S("evac_done"), evacs)
        for s in range(4):
            pe.wait_ge(S("lo_done"), slabs + s)
            for kt in range(4):
                k = 4 * s + kt
                for m in range(4):
                    at = slice(kt * 512 + m * P, kt * 512 + (m + 1) * P)
                    last = three(PS[:, 2 * par + m // 2, (m % 2) * T:(m % 2 + 1) * T],
                                 (whi[:, s % 2, at], wlo[:, s % 2, at]), Hhi[:, k, :], Hlo[:, k, :],
                                 first=(k == 0 and m % 2 == 0), last=(k == KT - 1))
            last.then_inc(S("slab_used"), 1)

    class Seg:
        pass
    plan = []
    cB = cG = cE = cQ = cN = 0

    def seg(name, bodies, src, split=True, ada=None, evacs=0, half=0):
        nonlocal cB, cG, cE, cQ, cN
        s = Seg()
        s.name, s.bodies, s.src, s.split, s.ada = name, bodies, src, split, ada
        s.B, s.G, s.E, s.Q, s.N = cB, cG, cE, cQ, cN
        s.half = half
        cB += bodies
        cG += 4 * bodies * split
        cE += evacs
        cQ += 48 * (ada is not None)
        cN += ada is not None
        plan.append(s)
        return s

    def rows(w, n0=0):
        def src(i, s):
            return w[4 * s * P:(4 * s + 4) * P, bass.ds((i + n0) * 512, 512)].rearrange(
                "(a p) m -> p a m", p=P)
        return src

    def down(w, half):
        def src(i, s):
            return w[bass.ds((i * 8 + 2 * s) * P, 2 * P), half * 1024:(half + 1) * 1024].rearrange(
                "(a p) m -> p a m", p=P)
        return src

    w_in, w_out, w_glu = a["mix_w_in"][0], a["mix_w_out"][0], a["s5_w_glu"][0]
    plan_ada0 = [seg("ada", 0, None, ada=(0, c)) for c in range(2)]
    plan_in = [seg("block", 8, rows(w_in, 8 * c), ada=(1, c), evacs=8) for c in range(2)]
    plan_out = [seg("block", 4, rows(w_out), evacs=4)]
    plan_mlp = []
    for layer in range(2):
        adas = [(2, 0), (2, 1), (3, 0), (3, 1)] if layer == 0 else [None] * 4
        if layer == 1:
            plan_v = seg("mats", 4, lambda i, s: vmat[bass.ds(i * 4 + s, 1)].rearrange("o p m -> p (o m)"),
                         split=False)
            plan_o = seg("mats", 5, lambda i, s: omat[bass.ds(i * 4 + s, 1)].rearrange("o p m -> p (o m)"),
                         split=False)
            plan_glu = [seg("block", 4, rows(w_glu, 4 * c), evacs=4) for c in range(2)]
        up = [seg("block", 8, rows(a["mlp_w1"][layer], 8 * c), ada=adas[c], evacs=8) for c in range(2)]
        dn = [seg("down", 8, down(a["mlp_w2"][layer], h), ada=adas[2 + h], evacs=0, half=h) for h in range(2)]
        plan_mlp.append((up, dn))
    GALL = cG


    ROTW = acc[:, 0:128]
    COS = acc[:, 128:384]
    SIN = acc[:, 384:640]
    MASKS = acc[:, 640:2560].bitcast(I32).rearrange("p (m t) -> p m t", m=15)
    ROTT = HF[:, 4096:4608].rearrange("p (b t) -> p b t", b=2)
    Vn = HF[:, 0:2048].rearrange("p (h a e) -> p h a e", h=8, a=2)
    EA = HF[:, 2048:3072].rearrange("p (b c t) -> p b c t", b=2, c=2)
    AT = HF[:, 3072:3584].rearrange("p (b a t) -> p b a t", b=2, a=2)
    VH = PF[:, 4096:6144].rearrange("p (h a e) -> p h a e", h=8, a=2)
    LC = [PF[:, 2048:4096], PF[:, 12288:14336]]
    SCO = HF[:, 6144:8192].rearrange("p (d h t) -> p d h t", d=2, h=8)
    SCD = HF[:, 4096:6144].rearrange("p (x t) -> p x t", x=16)
    EX = HF[:, 0:4096].rearrange("p (b x) -> p b x", b=2)
    QH, FF_, FB_, IB_, GH = (PF[:, o * T:(o + 8) * T] for o in (24, 32, 40, 48, 56))
    OA, OB = PF[:, 0:2048], PF[:, 8192:10240]
    mx, nm, sm, rc = ([small[:, 32 + 4 * k + 2 * p:34 + 4 * k + 2 * p] for p in range(2)] for k in range(4))
    HS = HF[:, 0:4096].rearrange("p (k j n) -> p k j n", k=16, j=4)
    UT = HF[:, 4096:8192].rearrange("p (t n) -> p t n", t=64)
    YT = HF[:, 0:4096].rearrange("p (t n) -> p t n", t=64)
    GF = PF[:, 0:4096].rearrange("p (k j n) -> p k j n", k=16, j=4)
    SV = PF[:, :].rearrange("p (n c x) -> p n c x", c=2, x=128)
    STP = acc[:, 0:512].rearrange("p (a c x) -> p a c x", a=2, c=2)
    ON = PF[:, 0:4096].rearrange("p (a d) -> p a d", a=2)
    XAB = small[:, 0:32].rearrange("p (a k) -> p a k", a=2)
    ZERO2 = small[:, 62:64]

    LNS = HF[:, 7936:8192]
    SQ, RS = HF[:, 0:2048], HF[:, 2048:4096]

    Rp = WF[:, 0:2048].rearrange("p (c x m) -> p c x m", c=2, x=8)
    LT = LTMP

    def pad(eng, lk, dst, tmps, pw, w, x, slots, signs):
        shape = [P, 8, slots, 16]
        pr, pi, q = (pw[:, k, bass.ds(x, 8), :].unsqueeze(3).broadcast_to(shape) for k in signs)
        wr, wi = (w[:, k, bass.ds(x, 8), :].unsqueeze(2).broadcast_to(shape) for k in range(2))
        t0, t1 = (tmps[:, k, 0:8 * slots * 16].rearrange("p (x s h) -> p x s h", s=slots, h=16)
                  for k in range(2))
        for c in range(2):
            settle(eng)
            lk(eng.tensor_tensor(t0, (pr, q)[c], (wr, wi)[c], ALU.mult))
            settle(eng)
            lk(eng.tensor_tensor(t1, pi, (wi, wr)[c], ALU.mult))
            for g in range(2):
                half = slice(64 * g, 64 * g + 64)
                lk(eng.tensor_tensor(dst[half, c, :, :, 16 * g:16 * g + 16], t0[half], t1[half],
                                     ALU.add if (c == 1 and slots == 4) else ALU.subtract))

    def stepper(eng, name, i, per):
        count = [0]

        def lk(ins):
            count[0] += 1
            ins.then_inc(S(name), 1)
            eng.wait_ge(S(name), i * per + count[0])
        return lk

    def rms_pe(pe, sem_in, sem_out, n, src):
        pe.wait_ge(S(sem_in), n)
        for b in range(4):
            last = nc.tensor.matmul(PS[:, b, :], ones[:, 0:P], src[:, b * 512:(b + 1) * 512],
                                    start=True, stop=True)
        last.then_inc(S(sem_out), 1)

    with nc.Block() as block:
        @block.sync
        def _(sp):
            def load(dst, src, sem):
                sp.dma_start(dst, src).then_inc(S(sem), 16)

            for name in ("v_stored", "out_stored", "intra_stored"):
                sp.sem_inc(S(name), 16 * PRIME_MAT)
            sp.wait_ge(S("stg_zero"), 1)
            load(ident[:], a["ident"], "ld_const")
            load(STG[0:96, 0, :], a["ada_b"].rearrange("l s (m p) -> (l s m) p", p=P)[0:96], "ld_par")
            load(STG[0:96, 1, :], a["ada_b"].rearrange("l s (m p) -> (l s m) p", p=P)[96:192], "ld_par")
            load(STG[0:64, 2, :], a["ln_g"].rearrange("l s (m p) -> (l s m) p", p=P), "ld_par")
            load(STG[64:128, 2, :], a["ln_b"].rearrange("l s (m p) -> (l s m) p", p=P), "ld_par")
            load(STG[0:16, 3, :], a["c"].rearrange("b (m p) -> (b m) p", p=P), "ld_par")
            load(STG[16:64, 3, :], a["hg_lower_bound"].rearrange("d l (m p) -> (d l m) p", p=P), "ld_par")
            load(STG[64:65, 3, :], a["diff_subln_g"], "ld_par")
            load(STG[65:66, 3, :], a["hg_norm_g"], "ld_par")
            load(LAMR, a["diff_lambda"][0].partition_broadcast(P), "ld_par")
            load(XN, a["x"][0].rearrange("(a p) d -> p a d", p=P), "ld_x")
            for d in range(2):
                load(LS[0:64, d, :], a["s5_lambda_re"][0, d].rearrange("(t g) p -> t (g p)", g=2), "ld_s5")
                load(LS[0:64, 2 + d, :], a["s5_lambda_im"][0, d].rearrange("(t g) p -> t (g p)", g=2), "ld_s5")
                load(LDT[0:64, d, :], a["s5_log_dt"][0, d].rearrange("(t g) -> t g", g=2), "ld_s5")
            for j in range(4):
                load(DST[0:64, j, :], a["s5_d"][0].rearrange("(t c) -> t c", c=32), "ld_s5")
            for c, (bn, cn) in enumerate((("s5_b_re", "s5_c_re"), ("s5_b_im", "s5_c_im"))):
                for d in range(2):
                    bd = Bn[:, c].rearrange("p (k d t) h -> p d t k h", d=2, t=4)[:, d]
                    src = a[bn][0, d].rearrange("(k t g) p h -> t (g p) k h", g=2, t=4)
                    for t in range(4):
                        load(bd[:, t], src[t], "ld_b")
                    src = a[cn][0, d].rearrange("(T k g) h p -> k g h T p", g=2, k=8)
                    for k in range(8):
                        for g in range(2):
                            load(Cn[16 * k:16 * k + 16, 2 * d + c, :, 64 * g:64 * g + 64], src[k, g], "ld_c")
            for s in plan_ada0:
                with sp.Fori(0, 8) as i:
                    ada_loads(sp, i, s.Q, s.ada[0], s.ada[1])
            with sp.Fori(0, 4) as q:
                for j in range(4):
                    sp.wait_ge(S("pad_ready"), q * 8 + (2 * j + 2))
                    for d in range(2):
                        for c in range(2):
                            sp.dma_start(
                                omat[bass.ds(q * 5 + (1 + j), 1), :, (2 * d + c) * 512:(2 * d + c + 1) * 512]
                                .rearrange("o p (t m) -> p (o t) m", t=4),
                                Op[:, c, 4 * d:4 * d + 4, 1 - d:5 - d, :].rearrange("p t s m -> p t (s m)")
                            ).then_inc(S("out_stored"), 16)
                    sp.wait_ge(S("vs_ready"), q * 4 + (j + 1 + PRIME_MAT))
                    sp.dma_start(vmat[bass.ds(q * 4 + j, 1)].rearrange("o p m -> p (o m)"),
                                 WF[:, 2048:4096]).then_inc(S("v_stored"), 16)
                sp.wait_ge(S("intra_ready"), q * 4 + (4 + PRIME_MAT))
                sp.dma_start(omat[bass.ds(q * 5, 1)].rearrange("o p m -> p (o m)"),
                             PF[:, 0:2048]).then_inc(S("intra_stored"), 16)

            def stream(s):
                with sp.Fori(0, s.bodies) as i:
                    slab_loads(sp, i, s.B, s.G, s.src)
                    if s.ada:
                        ada_loads(sp, i, s.Q, s.ada[0], s.ada[1])

            for s in plan_in:
                stream(s)
            sp.wait_ge(S("ada_freed"), 4)
            load(ROTW, a["rot"], "ld_rot")
            load(COS, a["cos"], "ld_rot")
            load(SIN, a["sin"], "ld_rot")
            load(acc[:, 640:2560].rearrange("p (m t) -> p m t", m=15), a["masks"].rearrange("m s t -> s m t"), "ld_rot")
            for s in plan_out:
                stream(s)
            for layer in range(2):
                if layer == 1:
                    sp.wait_ge(S("hs_ready"), 1)
                    for j in range(4):
                        for q in range(4):
                            sp.dma_start(UT[32 * j:32 * j + 32].rearrange("p (k a) n -> p a k n", a=4)[:, q],
                                         HS[32 * q:32 * q + 32, :, j, :]).then_inc(S("u_ready"), 16)
                    sp.wait_ge(S("v_stored"), 256 + 16 * PRIME_MAT)
                    sp.wait_ge(S("out_stored"), 1024 + 16 * PRIME_MAT)
                    sp.wait_ge(S("intra_stored"), 64 + 16 * PRIME_MAT)
                    for n in range(36):
                        if n < 4:
                            sp.wait_ge(S("lo_done"), plan_v.G + n + 1)
                        else:
                            sp.wait_ge(S("mat_used"), n - 3)
                        sp.dma_start(raw[:, n % 4, :], vmat[n] if n < 16 else omat[n - 16]
                                     ).then_inc(S(f"raw_ready{n % 4}"), 16)
                    sp.wait_ge(S("y_ready"), 1)
                    for j in range(4):
                        for q in range(4):
                            sp.dma_start(GF[32 * q:32 * q + 32, :, j, :],
                                         YT[32 * j:32 * j + 32].rearrange("p (k a) n -> p a k n", a=4)[:, q]
                                         ).then_inc(S("g_ready"), 16)
                    sp.wait_ge(S("mat_used"), 36)
                    for s in plan_glu:
                        stream(s)
                up, dn = plan_mlp[layer]
                for s in up + dn:
                    stream(s)
            for t in range(2):
                sp.wait_ge(S("out_ready"), t + 1)
                sp.dma_start(out[0].rearrange("(a p) d -> p a d", p=P)[:, t, :],
                             ON[:, t, :]).then_inc(S("stored"), 16)
            sp.wait_ge(S("stored"), 32)

        @block.tensor
        def _(pe):
            pe.sem_inc(S("slab_used"), PRIME_USED)
            pe.sem_inc(S("taps"), PRIME_MAT)
            pe.wait_ge(S("ld_const"), 16)
            pe.wait_ge(S("ld_par"), 9 * 16)
            pe.wait_ge(S("ones_ready"), 1)
            for t in range(4):
                last = nc.tensor.transpose(PS[:, 6, t * P:(t + 1) * P], STG[:, t, :], ident[:])
            last.then_inc(S("par_T"), 1)
            pe.wait_ge(S("ld_x"), 16)
            for kt in range(KT):
                if kt % 2 == 0 and kt >= 8:
                    pe.wait_ge(S("x_evac"), kt // 2 - 3)
                for t in range(2):
                    o = (kt % 2) * T + t * P
                    last = nc.tensor.transpose(PS[:, (kt // 2) % 4, o:o + P],
                                               XN[:, t, kt * P:(kt + 1) * P], ident[:])
                if kt % 2:
                    last.then_inc(S("x_T"), 1)
            for n, s in enumerate(plan_ada0):
                ada_sum_pe(pe, s.N, s.Q + 48, 7)
                pe.wait_ge(S("ada_freed"), n + 1)
            pe.wait_ge(S("ls_ready"), 1)
            for t in range(6):
                nc.tensor.transpose(PS[:, 5, t * 64:(t + 1) * 64], LS[0:64, t, :], ident[0:64, 0:64])
            nc.tensor.transpose(PS[:, 5, 384:448], DST[0:64].rearrange("p a c -> p (a c)"), ident[0:64, 0:64]
                                ).then_inc(S("ls_T"), 1)
            pe.wait_ge(S("ld_c"), 64 * 16)
            pe.wait_ge(S("x_evac"), 8)
            for n in range(8):
                if n >= 4:
                    pe.wait_ge(S("c_evac"), n - 3)
                for t in range(4):
                    last = nc.tensor.transpose(PS[:, n % 4, t * P:(t + 1) * P], Cn[:, n // 2, 4 * (n % 2) + t, :],
                                               ident[:])
                last.then_inc(S("c_T"), 1)
            pe.wait_ge(S("c_evac"), 8)
            pe.wait_ge(S("ls_evac"), 1)
            with pe.Fori(0, 16) as n:
                pe.wait_ge(S("pad_ready"), n * 2 + 2)
                pe.wait_ge(S("vs_ready"), n + PRIME_MAT)
                for d in range(2):
                    for c in range(2):
                        for t in range(4):
                            last = nc.tensor.transpose(PS[:, 2 * d + c, t * P:(t + 1) * P],
                                                       Vp[:, c, 4 * d + t].rearrange("p s m -> p (s m)"), ident[:])
                last.then_inc(S("v_T"), 1)
                pe.wait_ge(S("intra_ready"), n + PRIME_MAT)
                pe.wait_ge(S("rp_ready"), n + 1)
                for d in range(2):
                    for t in range(4):
                        for c in range(2):
                            last = nc.tensor.matmul(
                                PS[:, 4 + d, t * P:(t + 1) * P], Rp[:, c, 4 * d + t, :],
                                Op[:, c, 4 * d + t, d:d + 4, :].rearrange("p s m -> p (s m)"),
                                start=(c == 0), stop=(c == 1))
                last.then_inc(S("taps"), 1)

            def run_block(s, h=0):
                if h:
                    pe.wait_ge(S("h_ready"), h)
                with pe.Fori(0, s.bodies // 2) as i:
                    for par in range(2):
                        block_products(pe, i * 2 + (s.E + par + 1), i * 8 + (s.G + 4 * par + 1 + PRIME_RAW), par)
                if s.ada:
                    ada_sum_pe(pe, s.N, s.Q + 48, 4)

            def run_down(s, n):
                b0 = 4 * s.half
                if s.half:
                    pe.wait_ge(S("ada_freed"), s.ada_before)
                for b in range(b0, b0 + 4):
                    nc.tensor.matmul(PS[:, b, 0:2], ones[:, 0:P], ZERO2, start=True, stop=True,
                                     skip_group_check=True)
                with pe.Fori(0, 8) as i:
                    for sl in range(4):
                        pe.wait_ge(S("lo_done"), i * 4 + (s.G + sl + 1 + PRIME_RAW))
                        pe.wait_ge(S("hx_lo"), i * 4 + (n * 32 + sl + 1))
                        for kt in range(2):
                            k = 2 * (sl % 2) + kt
                            for m in range(8):
                                at = slice(kt * 1024 + m * P, kt * 1024 + (m + 1) * P)
                                last = three(PS[:, b0 + m // 2, (m % 2) * T:(m % 2 + 1) * T],
                                             (whi[:, sl % 2, at], wlo[:, sl % 2, at]),
                                             Hhi[:, k, :], Hlo[:, k, :], first=False, last=True)
                        last.then_inc(S("slab_used"), 1)
                if s.ada:
                    if s.half:
                        pe.wait_ge(S("down_evac"), n)
                    ada_sum_pe(pe, s.N, s.Q + 48, 4 if s.half == 0 else 0)

            def layer_norm_pe(k):
                pe.wait_ge(S("ln_sum"), 2 * k + 1)
                nc.tensor.matmul(PS[:, 4, 0:T], ones[:, 0:P], LNS, start=True, stop=True).then_inc(S("ln_psum"), 1)
                pe.wait_ge(S("ln_sum"), 2 * k + 2)
                nc.tensor.matmul(PS[:, 4, T:2 * T], ones[:, 0:P], LNS, start=True, stop=True).then_inc(S("ln_psum"), 1)

            def attention_pe():
                pe.wait_ge(S("in_done"), 1)
                for w in range(2):
                    for g in range(4):
                        if w == 1:
                            pe.wait_ge(S("vt_evac"), g + 1)
                        for x in range(4):
                            h, t = 2 * g + x // 2, x % 2
                            last = nc.tensor.transpose(PS[:, g, x * P:(x + 1) * P],
                                                       Pb[:, (16 if w == 0 else 48) + h, t * P:(t + 1) * P], ident[:])
                        last.then_inc(S("vt_T"), 1)
                pe.wait_ge(S("ld_rot"), 64)
                for n in range(8):
                    if n >= 2:
                        pe.wait_ge(S("rot_done"), n - 1)
                    nc.tensor.matmul(PS[:, 6 + n % 2, :], ROTW, PF[:, n * 512:(n + 1) * 512], start=True, stop=True
                                     ).then_inc(S("rot_mm"), 1)
                pe.wait_ge(S("rot_done"), 8)
                pe.wait_ge(S("vt_evac"), 8)

                def scores(n):
                    h, qt = n // 2, n % 2
                    if n >= 2:
                        pe.wait_ge(S("at_exp"), n - 1)
                    for c in range(2):
                        last = nc.tensor.matmul(PS[:, 2 * (n % 2) + c, 0:T],
                                                Pb[64 * c:64 * c + 64, h, qt * P:(qt + 1) * P],
                                                Pb[64 * c:64 * c + 64, 8 + h, :], start=True, stop=True)
                    last.then_inc(S("at_score"), 1)

                def values(n):
                    h, par = n // 2, n % 2
                    pe.wait_ge(S("at_mix"), n + 1)
                    for kt in range(2):
                        last = nc.tensor.transpose(PS[:, 4 + par, kt * P:(kt + 1) * P],
                                                   EA[:, par, 0, kt * P:(kt + 1) * P], ident[:])
                    last.then_inc(S("at_T"), 1)
                    pe.wait_ge(S("at_Te"), n + 1)
                    for kt in range(2):
                        last = nc.tensor.matmul(PS[:, 6 + par, 0:P], Vn[:, h, kt, :], AT[:, par, kt, :],
                                                start=(kt == 0), stop=(kt == 1))
                    last.then_inc(S("at_pv"), 1)

                scores(0)
                for n in range(16):
                    if n < 15:
                        scores(n + 1)
                    values(n)
                rms_pe(pe, "rms_sq", "rms_sum", 1, SQ)

            def hgrn_pe():
                for n in range(17):
                    lv, d = n // 2, n % 2
                    b0 = 4 * (n % 2)
                    pe.wait_ge(S("lv_x"), n + 1)
                    if n >= 2:
                        pe.wait_ge(S("lv_put"), n - 1)
                    e = EX[:, n % 2].rearrange("p (h t) -> p h t", h=8)
                    for h in range(8):
                        for t in range(2):
                            x = e[:, h, t * P:(t + 1) * P]
                            if lv == 7 and t == 0:
                                y = e[:, h, P:2 * P]
                                last = nc.tensor.matmul(PS[:, b0 + h // 4, (h % 4) * P:(h % 4 + 1) * P],
                                                        x if d == 0 else y, y if d == 0 else x, start=True, stop=True)
                            elif lv != 7:
                                y = x if lv < 8 else QH.rearrange("p (h t) -> p h t", h=8)[:, h, t * P:(t + 1) * P]
                                z = 2 * h + t
                                last = nc.tensor.matmul(PS[:, b0 + z // 4, (z % 4) * P:(z % 4 + 1) * P],
                                                        x, y, start=True, stop=True)
                    last.then_inc(S("lv_mm"), 1)
                pe.wait_ge(S("lv_put"), 17)
                for h in range(8):
                    for t in range(2):
                        ps = PS[:, 4 + h // 2, (h % 2) * T + t * P:(h % 2) * T + (t + 1) * P]
                        nc.tensor.matmul(ps, VH[:, h, t], SCD[:, 2 * h + t], start=True, stop=False)
                        last = nc.tensor.matmul(ps, VH[:, h, 1 - t], SCO[:, 1 - t, h], start=False, stop=True)
                last.then_inc(S("hg_pv"), 1)
                rms_pe(pe, "rms_sq", "rms_sum", 2, SQ)

            def s5_pe():
                pe.wait_ge(S("u_ready"), 256)
                B = plan_v.B
                for n in range(36):
                    pe.wait_ge(S(f"raw_ready{n % 4}"), (B + n // 4 + 1) * 16)
                    mats = raw[:, n % 4, :].rearrange("p (x m) -> p x m", x=16)
                    if n < 16:
                        if n >= 4:
                            pe.wait_ge(S("sv_evac"), n - 3)
                        for d in range(2):
                            for c in range(2):
                                for t in range(4):
                                    o = d * 4 + t
                                    u = UT[:, 4 * n + t, :] if d == 0 else UT[:, 4 * n + t, ::-1]
                                    last = nc.tensor.matmul(
                                        PS[:, 2 * (n % 4) + c, o * 64:(o + 1) * 64],
                                        mats[:, 8 * d + 4 * c + t], u, start=True, stop=True)
                    else:
                        q, j = (n - 16) // 5, (n - 16) % 5
                        if j == 0:
                            if q == 0:
                                pe.wait_ge(S("sv_evac"), 16)
                            for t in range(16):
                                last = nc.tensor.matmul(PS[:, 2 * q + t // 8, (t % 8) * 64:(t % 8 + 1) * 64],
                                                        mats[:, t], UT[:, 16 * q + t, :], start=(t % 8 == 0),
                                                        stop=False, skip_group_check=True)
                        else:
                            pe.wait_ge(S("s5_scan"), 1)
                            for d in range(2):
                                for c in range(2):
                                    for t in range(4):
                                        tt = 4 * (j - 1) + t
                                        x = 8 * (4 * q + j - 1) + 4 * d + t
                                        st = SV[:, 0:63, c, x] if d == 0 else SV[:, 62::-1, c, x]
                                        o = (tt % 8) * 64 + (1 - d)
                                        last = nc.tensor.matmul(PS[:, 2 * q + tt // 8, o:o + 63],
                                                                mats[:, 8 * d + 4 * c + t], st, start=False,
                                                                stop=True, skip_group_check=True)
                    last.then_inc(S("mat_used"), 1)

            for n, s in enumerate(plan_in):
                run_block(s, 1 if n == 0 else 0)
            attention_pe()
            hgrn_pe()
            for s in plan_out:
                run_block(s, 2)
            layer_norm_pe(0)
            for layer in range(2):
                if layer == 1:
                    s5_pe()
                    for n, s in enumerate(plan_glu):
                        run_block(s, 4 if n == 0 else 0)
                    layer_norm_pe(2)
                up, dn = plan_mlp[layer]
                for n, s in enumerate(up):
                    run_block(s, (3 if layer == 0 else 5) if n == 0 else 0)
                pe.wait_ge(S("evac_done"), up[1].E + 8 + PRIME_EVAC)
                for s in dn:
                    s.ada_before = dn[0].N + 1 if s.ada else up[0].N
                    run_down(s, 2 * layer + s.half)
                layer_norm_pe(1 + 2 * layer)
            pe.wait_ge(S("x_final"), 1)
            for t in range(2):
                for g in range(4):
                    for x in range(4):
                        kt = 4 * g + x
                        last = nc.tensor.transpose(PS[:, 4 * t + g, x * P:(x + 1) * P],
                                                   X[:, kt, t * P:(t + 1) * P], ident[:])
                    last.then_inc(S("o_T"), 1)

        @block.scalar
        def _(act):
            link = chain(act, "act_chain")
            act.sem_inc(S("evac_done"), PRIME_EVAC)
            act.sem_inc(S("vs_ready"), PRIME_MAT)

            def run(out_, in_, func=ACT.Copy, sem=None, **kw):
                ins = nc.scalar.activation(out_, in_, func, **kw)
                if sem:
                    ins.then_inc(S(sem), 1)
                return ins

            act.wait_ge(S("par_ready"), 1)
            run(cact[:], CRAW, ACT.Sigmoid)
            run(TP[:, 0, 0:48], TP[:, 0, 0:48], ACT.Exp)
            run(TP[:, 0, 128:130], TP[:, 0, 128:130], ACT.Exp, "par_act")
            for n in range(8):
                act.wait_ge(S("x_T"), n + 1)
                run(X[:, 2 * n:2 * n + 2, :], PS[:, n % 4, :].rearrange("p (a t) -> p a t", a=2), sem="x_evac")
            for n in range(8):
                act.wait_ge(S("c_T"), n + 1)
                ci, T2 = n // 2, n % 2
                d, c = ci // 2, ci % 2
                dst = HF[:, 2048 * c:2048 * c + 2048].rearrange("p (k d x) -> p d k x", d=2, x=64)
                run(dst[:, d, 8 * T2:8 * T2 + 8, :], PS[:, n % 4, :].rearrange("p (k x) -> p k x", x=64), sem="c_evac")
            act.wait_ge(S("s5_dt"), 1)
            run(TM[:, 2], TM[:, 2], ACT.Exp, "s5_act")
            act.wait_ge(S("s5_dt"), 2)
            run(TM[:, 3], TM[:, 3], ACT.Exp)
            run(TM[:, 6:8], TM[:, 6:8], ACT.Sin, "s5_act")
            with act.Fori(0, 4) as q:
                act.wait_ge(S("intra_stored"), q * 16 + 16 * PRIME_MAT)
                for j in range(4):
                    act.wait_ge(S("pad_ready"), q * 8 + (2 * j + 2))
                    act.wait_ge(S("taps"), q * 4 + (j + PRIME_MAT))
                    for c in range(2):
                        for d in range(2):
                            src = Vp[:, c, 4 * d:4 * d + 4, 3 * (1 - d), :]
                            ins = run(Rp[:, c, 4 * d:4 * d + 4].rearrange("p t (r m) -> p t r m", r=4),
                                      src.unsqueeze(2).broadcast_to([P, 4, 4, 32]))
                    ins.then_inc(S("rp_ready"), 1)
                    act.wait_ge(S("v_T"), q * 4 + (j + 1))
                    act.wait_ge(S("v_stored"), q * 64 + 16 * (j + PRIME_MAT))
                    run(WF[:, 2048:4096], bank(0, 4), sem="vs_ready")
                    act.wait_ge(S("taps"), q * 4 + (j + 1 + PRIME_MAT))
                    for r in range(4):
                        rows_ = slice(32 * r, 32 * r + 32)
                        ins = run(INTRA[rows_, 4 * j:4 * j + 4, 32 * r:P],
                                  PS[rows_, 4, :].rearrange("p (t m) -> p t m", t=4)[:, :, 0:(4 - r) * 32])
                    ins.then_inc(S("intra_f"), 1)

            def h_hi(n, src):
                for g in range(4):
                    act.wait_ge(S("h32"), 4 * n + g + 1)
                    run(Hhi[:, 4 * g:4 * g + 4, :], src[:, 1024 * g:1024 * g + 1024]
                        .rearrange("p (a t) -> p a t", a=4), sem="h_hi")

            def evac(s, blk, par):
                act.wait_ge(S("slab_used"), blk * 4 + (s.G + 4 + PRIME_USED))
                dst = Pb[:, bass.ds(blk * 4 + s.tile0, 4), :]
                src = PS[:, 2 * par:2 * par + 2, :].rearrange("p b (m t) -> p (b m) t", t=T)
                settle(act)
                run(dst, src, s.func, sem="evac_done")
                if s.func == ACT.Relu:
                    act.wait_ge(S("evac_done"), blk + (s.E + 1 + PRIME_EVAC))
                    settle(act)
                    run(dst, dst, ACT.Square, sem="sq_done")

            def blocks(segs):
                prev = None
                for s in segs:
                    def body(blk, par, before):
                        for sl in range(4):
                            split_hi(act, blk, s.B, s.G, sl)
                            if sl == 1 and before is not None:
                                evac(*before, 1 - par)
                    for blk in range(2):
                        body(blk, blk, prev)
                        prev = (s, blk)
                    with act.Fori(1, s.bodies // 2) as i:
                        for par in range(2):
                            body(i * 2 + par, par, (s, i * 2 + (par - 1)))
                    prev = (s, s.bodies - 1)
                evac(*prev, 1)

            def down_hi(s, n):
                with act.Fori(0, 8) as i:
                    for sl in range(4):
                        split_hi(act, i, s.B, s.G, sl)
                        run(Hhi[:, 2 * (sl % 2):2 * (sl % 2) + 2, :], Pb[:, bass.ds(i * 8 + 2 * sl, 2), :],
                            sem="hx_hi")

            def layer_norm_act(k):
                act.wait_ge(S("ln_cent"), k + 1)
                run(PF[:, 0:4096], X[:].rearrange("p k t -> p (k t)"), ACT.Square, "ln_sq")
                act.wait_ge(S("ln_psum"), 2 * k + 2)
                run(LNS, PS[:, 4, T:2 * T], ACT.Sqrt, "ln_std", scale=1.0 / D, bias=eps[:, 0:1])

            def rms_act(n, o):
                run(SQ, o, ACT.Square, "rms_sq")
                act.wait_ge(S("rms_sum"), n)
                run(RS, bank(0, 4), ACT.Sqrt, "rms_std", scale=1.0 / P, bias=eps[:, 1:2])

            def attention_act():
                for g in range(8):
                    act.wait_ge(S("vt_T"), g + 1)
                    dst = (HF[:, 0:2048] if g < 4 else PF[:, 4096:6144])[:, 512 * (g % 4):512 * (g % 4) + 512]
                    run(dst, PS[:, g % 4, :], sem="vt_evac")

                def exps(n):
                    par = n % 2
                    act.wait_ge(S("at_max"), n + 1)
                    if n >= 2:
                        act.wait_ge(S("at_T"), n - 1)
                    for c in range(2):
                        ins = run(EA[:, par, c, :], PS[:, 2 * par + c, 0:T], ACT.Exp, scale=QK_SCALE,
                                  bias=nm[par][:, c:c + 1], accum_out=sm[par][:, c:c + 1])
                    ins.then_inc(S("at_exp"), 1)

                exps(0)
                for n in range(16):
                    h, qt, par = n // 2, n % 2, n % 2
                    if n < 15:
                        exps(n + 1)
                    act.wait_ge(S("at_T"), n + 1)
                    run(AT[:, par], PS[:, 4 + par, 0:T].rearrange("p (a t) -> p a t", a=2), sem="at_Te")
                    act.wait_ge(S("at_pv"), n + 1)
                    link(run(Pb[:, h, qt * P:(qt + 1) * P], PS[:, 6 + par, 0:P]))
                rms_act(1, OA)

            def hgrn_act():
                act.wait_ge(S("oa_final"), 1)
                run(EX[:, 0], QH, ACT.Sigmoid)
                run(EX[:, 1], GH, ACT.Sigmoid, "hg_sig")
                run(PF[:, 8192:12288], PF[:, 8192:12288], ACT.Sigmoid, "hg_sig")
                for d in range(2):
                    act.wait_ge(S("hg_f"), d + 1)
                    run(EX[:, d], EX[:, d], ACT.Ln, "hg_ln")
                for n in range(16):
                    act.wait_ge(S("lv_arg"), n + 1)
                    run(EX[:, n % 2], EX[:, n % 2], ACT.Exp, "lv_exp")
                act.wait_ge(S("hg_pv"), 1)
                link(run(OB, bank(4, 4)))
                rms_act(2, OB)
                act.wait_ge(S("o_ready"), 1)
                run(Hhi[:, 0:8, :], Pb[:, 0:8, :], sem="o_hi")
                run(Hhi[:, 8:16, :], Pb[:, 32:40, :], sem="o_hi")

            def s5_act():
                for n in range(16):
                    act.wait_ge(S("mat_used"), n + 1)
                    for c in range(2):
                        ins = run(SV[:, :, c, 8 * n:8 * n + 8].rearrange("p n x -> p x n"),
                                  PS[:, 2 * (n % 4) + c, :].rearrange("p (x n) -> p x n", x=8))
                    ins.then_inc(S("sv_evac"), 1)
                act.wait_ge(S("ge_in"), 1)
                run(PF[:, 8192:12288], HF[:, 0:4096], ACT.Square, "ge_sq")
                act.wait_ge(S("ge_in"), 2)
                run(PF[:, 8192:12288], PF[:, 8192:12288], ACT.Sigmoid, "ge_sig", scale=2 * GELU_C)
                act.wait_ge(S("g_ready"), 256)
                run(Hhi[:].rearrange("p k t -> p (k t)"), PF[:, 0:4096], sem="o_hi")

            h_hi(0, PF[:, 4096:8192])
            for s in plan_in:
                s.func, s.tile0 = ACT.Copy, 4 * (s.E - plan_in[0].E)
            blocks(plan_in)
            act.wait_ge(S("evac_done"), PRIME_EVAC + 16)
            act.sem_inc(S("in_done"), 1)
            attention_act()
            hgrn_act()
            for s in plan_out:
                with act.Fori(0, s.bodies) as i:
                    for sl in range(4):
                        split_hi(act, i, s.B, s.G, sl)
            layer_norm_act(0)
            h_hi(1, PF[:, 4096:8192])
            for layer in range(2):
                if layer == 1:
                    s5_act()
                    for n, s in enumerate(plan_glu):
                        s.func, s.tile0 = (ACT.Copy, ACT.Sigmoid)[n], 16 + 16 * n
                    blocks(plan_glu)
                    layer_norm_act(2)
                    h_hi(2, PF[:, 4096:8192])
                up, dn = plan_mlp[layer]
                for n, s in enumerate(up):
                    s.func, s.tile0 = ACT.Relu, 32 * n
                blocks(up)
                act.wait_ge(S("sq_done"), 16 * (layer + 1))
                for s in dn:
                    down_hi(s, 2 * layer + s.half)
                layer_norm_act(1 + 2 * layer)
            for n in range(8):
                act.wait_ge(S("o_T"), n + 1)
                ins = run(ON[:, n // 4, (n % 4) * 512:(n % 4 + 1) * 512], PS[:, n, :])
                if n % 4 == 3:
                    ins.then_inc(S("out_ready"), 1)

        @block.vector
        def _(v):
            link = chain(v, "dve_chain")
            tt, ts, stt = nc.vector.tensor_tensor, nc.vector.tensor_scalar, nc.vector.scalar_tensor_tensor
            v.sem_inc(S("lo_done"), PRIME_RAW)
            v.sem_inc(S("intra_ready"), PRIME_MAT)
            v.sem_inc(S("ada_used"), PRIME_ADA)
            link(nc.vector.memset(WF[:, 0:512], 0.0))
            v.sem_inc(S("stg_zero"), 1)
            for ap, x in ((ones[:], 1.0), (small[:], 0.0), (eps[:, 0:1], LN_EPS), (eps[:, 1:2], RMS_EPS),
                          (acc[:], 0.0), (PF[:, 4096:6144], 0.0), (WF[:, 4096:6656], 0.0)):
                link(nc.vector.memset(ap, x))
            v.sem_inc(S("ones_ready"), 1)
            v.wait_ge(S("par_T"), 1)
            link(nc.vector.tensor_copy(PT[:].rearrange("p a c -> p (a c)"), PS[:, 6, :]))
            lb3 = LBR.rearrange("p (d l m) -> p l d m", d=2, l=3)
            e3 = TP[:, 0, 0:48].rearrange("p (l d m) -> p l d m", l=3, d=2)
            m3 = TP[:, 0, 64:80].rearrange("p (d m) -> p d m", d=2)
            link(tt(m3, lb3[:, 0], lb3[:, 1], ALU.max))
            link(tt(m3, m3, lb3[:, 2], ALU.max))
            for l in range(3):
                link(tt(e3[:, l], lb3[:, l], m3, ALU.subtract))
            v.wait_ge(S("ld_par"), 9 * 16)
            for k in range(2):
                link(tt(LT[:, k], LAMR[:, 2 * k], LAMR[:, 2 * k + 1], ALU.mult))
            link(nc.vector.tensor_reduce(TP[:, 0, 128:130], LT, AX.X, ALU.add))
            v.sem_inc(S("par_ready"), 1)
            v.wait_ge(S("par_act"), 1)
            link(tt(cact[:], cact[:], CRAW, ALU.mult))
            link(tt(m3, e3[:, 0], e3[:, 1], ALU.add))
            link(tt(m3, m3, e3[:, 2], ALU.add))
            link(nc.vector.reciprocal(TP[:, 0, 64:80], TP[:, 0, 64:80]))
            link(tt(lbs[:, :, 0:8], e3[:, 0], m3, ALU.mult))
            link(ts(lbs[:, :, 8:16], lbs[:, :, 0:8], -1.0, 1.0, ALU.mult, ALU.add))
            link(tt(lamb[:, 1:2], TP[:, 0, 129:130], TP[:, 0, 128:129], ALU.subtract))
            link(ts(lamb[:, 0:1], lamb[:, 1:2], -LAM_INIT, None, ALU.add))
            link(ts(SUBG, SUBG, 1.0 - LAM_INIT, None, ALU.mult))
            v.wait_ge(S("ld_s5"), 10 * 16)
            for d in range(2):
                link(nc.vector.tensor_copy(LS[0:64, 4 + d, :].rearrange("p (g x) -> p g x", g=2),
                                           LDT[0:64, d, :].unsqueeze(2).broadcast_to([64, 2, 64])))
            v.sem_inc(S("ls_ready"), 1)
            for s in plan_ada0:
                with v.Fori(0, 8) as i:
                    for r in range(6):
                        ada_mac(v, i, s.Q, r)
                ada_finish(v, link, s.N, s.ada[0], s.ada[1], 7)

            v.wait_ge(S("ls_T"), 1)
            for k in range(3):
                for d in range(2):
                    link(nc.vector.tensor_copy(
                        TM[:, k].rearrange("p (c d t) -> p d c t", d=2, t=4)[:, d],
                        PS[:, 5, (2 * k + d) * 64:(2 * k + d + 1) * 64].rearrange("p (c t) -> p c t", t=4)))
            link(nc.vector.tensor_copy(Dsk[:], PS[:, 5, 384:448]))
            v.sem_inc(S("ls_evac"), 1)
            v.sem_inc(S("s5_dt"), 1)
            LR, LI, DT, T3, T4, T5, T6, T7 = (TM[:, k] for k in range(8))
            v.wait_ge(S("s5_act"), 1)
            link(tt(T3, LR, DT, ALU.mult))
            link(tt(T4, LI, DT, ALU.mult))
            two_pi = 2 * math.pi
            c1 = float(np.float32(6.28125))
            c2 = float(np.float32(np.float32((two_pi - c1) * 2 ** 20).astype(np.int64) / 2 ** 20))
            c3 = two_pi - c1 - c2
            for dst, shift in ((T6, 0.0), (T7, 0.25)):
                link(ts(T5, T4, 1 / two_pi, shift, ALU.mult, ALU.add))
                link(ts(T5, T5, MAGIC, None, ALU.add))
                link(ts(T5, T5, -MAGIC, None, ALU.add))
                link(stt(dst, T5, -c1, T4, ALU.mult, ALU.add))
                link(stt(dst, T5, -c2, dst, ALU.mult, ALU.add))
                link(stt(dst, T5, -c3, dst, ALU.mult, ALU.add))
                if shift:
                    link(ts(dst, dst, math.pi / 2, None, ALU.add))
                pi_ = float(np.nextafter(np.float32(math.pi), np.float32(0)))
                link(ts(dst, dst, pi_, -pi_, ALU.min, ALU.max))
            v.sem_inc(S("s5_dt"), 1)
            v.wait_ge(S("s5_act"), 2)
            AR, AI = PW[:, 0, 0], PW[:, 0, 1]
            link(tt(AR, T3, T7, ALU.mult))
            link(tt(AI, T3, T6, ALU.mult))
            link(tt(T3, LR, LR, ALU.mult))
            link(tt(T4, LI, LI, ALU.mult))
            link(tt(T3, T3, T4, ALU.add))
            link(nc.vector.reciprocal(T3, T3))
            link(ts(T5, AR, -1.0, None, ALU.add))
            link(tt(T6, T5, LR, ALU.mult))
            link(tt(T7, AI, LI, ALU.mult))
            link(tt(T6, T6, T7, ALU.add))
            link(tt(T6, T6, T3, ALU.mult))
            link(tt(T7, AI, LR, ALU.mult))
            link(tt(T4, T5, LI, ALU.mult))
            link(tt(T7, T7, T4, ALU.subtract))
            link(tt(T7, T7, T3, ALU.mult))
            v.wait_ge(S("ld_b"), 256)
            bc = [t_.unsqueeze(2).broadcast_to([P, P, 16]) for t_ in (T6, T7)]
            tmp = PF[:, 0:2048].rearrange("p (x h) -> p x h", h=16)
            for c in range(2):
                link(tt(tmp, bc[1], Bn[:, 1 - c], ALU.mult))
                link(tt(BB[:, c], bc[0], Bn[:, c], ALU.mult))
                link(tt(BB[:, c], BB[:, c], tmp, ALU.subtract if c == 0 else ALU.add))
            for k in range(1, 4):
                pr, pi = PW[:, k - 1, 0], PW[:, k - 1, 1]
                link(tt(T3, pr, AR, ALU.mult))
                link(tt(T4, pi, AI, ALU.mult))
                link(tt(PW[:, k, 0], T3, T4, ALU.subtract))
                link(tt(T3, pr, AI, ALU.mult))
                link(tt(T4, pi, AR, ALU.mult))
                link(tt(PW[:, k, 1], T3, T4, ALU.add))
            for k, (c, f) in enumerate(((0, 1.0), (0, 1.0), (1, -1.0), (1, 1.0))):
                link(ts(A4[:, k, :], PW[:, 3, c], f, None, ALU.mult))
            v.wait_ge(S("c_evac"), 8)
            link(nc.vector.memset(PF[:, 10240:13184], 0.0))
            for e in range(5):
                for d in range(2):
                    for c in range(3):
                        def slot(arr, c_, k):
                            return arr[:, c_, :, k].rearrange("p (c d t) -> p d c t", d=2, t=4)[:, d]
                        spots = [slot(PWO, c, e if d == 0 else 4 - e)]
                        if c < 2 and e < 4:
                            spots.append(slot(PWV, c, 3 - e if d == 0 else e))
                        for sp_ in spots:
                            if e == 0:
                                if c != 1:
                                    link(nc.vector.memset(sp_, 1.0 if c == 0 else -1.0))
                            else:
                                link(ts(sp_, PW[:, e - 1, c % 2].rearrange("p (c d t) -> p d c t", d=2, t=4)[:, d],
                                        -1.0 if c == 2 else 1.0, None, ALU.mult))
            v.sem_inc(S("pw_ready"), 1)

            with v.Fori(0, 4) as q:
                lk = stepper(v, "v_steps", q, 4 * (8 + 7))
                for j in range(4):
                    pad(nc.vector, lk, Vp, TP, PWV, BB, q * 32 + 8 * j, 4, (0, 1, 0))
                    v.sem_inc(S("pad_ready"), 1)
                    v.wait_ge(S("taps"), q * 4 + (j + 1 + PRIME_MAT))
                    v.wait_ge(S("intra_f"), q * 4 + (j + 1))
                    ps = PS[:, 5, :].rearrange("p (t m) -> p t m", t=4)
                    for r in range(4):
                        R_ = slice(32 * r, 32 * r + 32)
                        tl = slice(4 * j, 4 * j + 4)
                        if r:
                            lk(nc.vector.tensor_copy(INTRA[R_, tl, 0:32 * r], ps[R_, :, (3 - r) * 32:96]))
                        lk(tt(INTRA[R_, tl, 32 * r:32 * r + 32], INTRA[R_, tl, 32 * r:32 * r + 32],
                              ps[R_, :, 96:128], ALU.add))
                    v.sem_inc(S("intra_ready"), 1)

            def modulation(sub, k):
                link(ts(G1[:, sub], MOD[:, sub, 32:48], 1.0, None, ALU.add))
                link(ts(HA[:, 0], MOD[:, sub, 16:32], 1.0, None, ALU.add))
                if k is None:
                    link(nc.vector.tensor_copy(HA[:, 1], MOD[:, sub, 0:16]))
                    link(nc.vector.memset(XAB[:, 0], ALPHA))
                    link(nc.vector.memset(XAB[:, 1], 0.0))
                else:
                    link(tt(HA[:, 1], HA[:, 0], LNB[k], ALU.mult))
                    link(tt(HA[:, 1], HA[:, 1], MOD[:, sub, 0:16], ALU.add))
                    link(tt(HA[:, 0], HA[:, 0], LNG[k], ALU.mult))
                    link(ts(XAB[:, 0], LNG[k], ALPHA, None, ALU.mult))
                    link(ts(XAB[:, 1], LNB[k], ALPHA, None, ALU.mult))
                v.sem_inc(S("xab_ready"), 1)

            h32 = PF[:, 4096:8192].rearrange("p (k t) -> p k t", t=T)

            def make_h(n, hn):
                for g in range(4):
                    for k in range(4):
                        kt = 4 * g + k
                        ins = ts(h32[:, kt], X[:, kt], HA[:, 0, kt:kt + 1], HA[:, 1, kt:kt + 1], ALU.mult, ALU.add)
                    ins.then_inc(S("h32"), 1)
                for g in range(4):
                    v.wait_ge(S("h_hi"), 4 * n + g + 1)
                    gs = slice(4 * g, 4 * g + 4)
                    link(tt(Hlo[:, gs], h32[:, gs], Hhi[:, gs].bitcast(F), ALU.subtract))
                v.sem_inc(S("h_ready"), 1)

            def layer_norm(k):
                link(nc.vector.tensor_reduce(LNS, X[:].rearrange("p k t -> p t k"), AX.X, ALU.add))
                v.sem_inc(S("ln_sum"), 1)
                v.wait_ge(S("ln_psum"), 2 * k + 1)
                link(stt(X[:], PS[:, 4, 0:T].unsqueeze(1).broadcast_to([P, KT, T]), -1.0 / D, X[:],
                         ALU.mult, ALU.add))
                v.sem_inc(S("ln_cent"), 1)
                v.wait_ge(S("ln_sq"), k + 1)
                link(nc.vector.tensor_reduce(LNS, PF[:, 0:4096].rearrange("p (k t) -> p t k", t=T), AX.X, ALU.add))
                v.sem_inc(S("ln_sum"), 1)
                v.wait_ge(S("ln_std"), k + 1)
                link(nc.vector.reciprocal(LNS, LNS))
                link(tt(X[:], X[:], LNS.unsqueeze(1).broadcast_to([P, KT, T]), ALU.mult))

            def split_lows(segs, fin=None, evac=None, down=None):
                for s in segs:
                    def body(i, first):
                        order = {0: [], 1: [], 2: [0, 1, 2], 3: [3, 4, 5]} if first else \
                                {0: [0, 1], 1: [2], 2: [3, 4], 3: [5]}
                        for sl in range(4):
                            split_lo(v, i, s.B, s.G, sl)
                            if down is not None:
                                v.wait_ge(S("hx_hi"), i * 4 + ((down + s.half) * 32 + sl + 1))
                                hs = slice(2 * (sl % 2), 2 * (sl % 2) + 2)
                                tt(Hlo[:, hs], Pb[:, bass.ds(i * 8 + 2 * sl, 2), :], Hhi[:, hs].bitcast(F),
                                   ALU.subtract).then_inc(S("hx_lo"), 1)
                            if first and sl == 1:
                                if down is not None and s.half:
                                    evac_down(segs[0], down)
                                if fin:
                                    ada_finish(v, link, fin.N, fin.ada[0], fin.ada[1],
                                               0 if fin.name == "down" and fin.half else 4)
                            if s.ada:
                                for r in order[sl]:
                                    ada_mac(v, i, s.Q, r)
                    body(0, True)
                    with v.Fori(1, s.bodies) as i:
                        body(i, False)
                    fin = s if s.ada else None
                return fin

            def evac_down(s, n):
                v.wait_ge(S("x_scaled"), n + 2)
                v.wait_ge(S("slab_used"), s.G + 32 + PRIME_USED)
                for m in range(8):
                    kt = 8 * s.half + m
                    ins = stt(X[:, kt], PS[:, 4 * s.half + m // 2, (m % 2) * T:(m % 2 + 1) * T],
                              G1[:, n + 1, kt:kt + 1], X[:, kt], ALU.mult, ALU.add)
                ins.then_inc(S("down_evac"), 1)
                v.wait_ge(S("down_evac"), n + s.half + 1)

            modulation(0, None)
            v.wait_ge(S("x_evac"), 8)
            v.wait_ge(S("v_stored"), 256 + 16 * PRIME_MAT)
            v.wait_ge(S("out_stored"), 1024 + 16 * PRIME_MAT)
            v.wait_ge(S("intra_stored"), 64 + 16 * PRIME_MAT)
            make_h(0, 1)
            fin = split_lows(plan_in)
            ada_finish(v, link, fin.N, fin.ada[0], fin.ada[1], 4)

            v.wait_ge(S("ld_rot"), 64)
            v.wait_ge(S("in_done"), 1)
            cs, sn = (z.unsqueeze(1).broadcast_to([P, 2, T]) for z in (COS, SIN))
            for n in range(8):
                v.wait_ge(S("rot_mm"), n + 1)
                qk = Pb[:, 2 * n:2 * n + 2, :]
                link(tt(ROTT, PS[:, 6 + n % 2, :].rearrange("p (b t) -> p b t", b=2), sn, ALU.mult))
                link(tt(qk, qk, cs, ALU.mult))
                link(tt(qk, qk, ROTT, ALU.add))
                v.sem_inc(S("rot_done"), 1)

            def row_max(n):
                par = n % 2
                v.wait_ge(S("at_score"), n + 1)
                link(nc.vector.tensor_reduce(mx[par], PS[:, 2 * par:2 * par + 2, 0:T], AX.X, ALU.max))
                link(ts(nm[par], mx[par], -QK_SCALE, None, ALU.mult))
                v.sem_inc(S("at_max"), 1)

            def mix(n):
                par = n % 2
                v.wait_ge(S("at_exp"), n + 1)
                link(nc.vector.reciprocal(rc[par], sm[par]))
                link(tt(rc[par][:, 1:2], rc[par][:, 1:2], lamb[:, 0:1], ALU.mult))
                link(ts(EA[:, par, 1], EA[:, par, 1], rc[par][:, 1:2], None, ALU.mult))
                link(stt(EA[:, par, 0], EA[:, par, 0], rc[par][:, 0:1], EA[:, par, 1], ALU.mult, ALU.add))
                v.sem_inc(S("at_mix"), 1)

            row_max(0)
            for n in range(16):
                if n < 15:
                    row_max(n + 1)
                mix(n)
            v.wait_ge(S("rms_std"), 1)
            link(nc.vector.reciprocal(RS, RS))
            link(stt(OA, OA, SUBG, RS, ALU.mult, ALU.mult))
            v.sem_inc(S("oa_final"), 1)

            link(nc.vector.memset(HF[:, 4096:6144], 0.0))
            v.wait_ge(S("hg_sig"), 1)
            link(tt(QH, QH, EX[:, 0], ALU.mult))
            link(tt(GH, GH, EX[:, 1], ALU.mult))
            v.wait_ge(S("hg_sig"), 2)
            for d, ff in enumerate((FF_, FB_)):
                for h in range(8):
                    hs = slice(h * T, (h + 1) * T)
                    link(ts(EX[:, d, hs], ff[:, hs], lbs[:, d, 8 + h:9 + h], lbs[:, d, h:h + 1], ALU.mult, ALU.add))
                link(ts(ff, EX[:, d], -1.0, 1.0, ALU.mult, ALU.add))
                v.sem_inc(S("hg_f"), 1)
            for d in range(2):
                v.wait_ge(S("hg_ln"), d + 1)
                if d:
                    link(nc.vector.memset(LC[1].rearrange("p (h t) -> p h t", h=8)[:, :, 0:1], 0.0))
                for h in range(8):
                    link(nc.vector.tensor_tensor_scan(LC[d][:, h * T + d:(h + 1) * T], ones[:, 0:T - d],
                                                      EX[:, d, h * T:(h + 1) * T - d], 0.0, ALU.mult, ALU.add))

            def level_views(ap, half):
                z = ap.rearrange("p (b u q) -> p u b q", u=2, q=half)
                return z[:, 0], z[:, 1]

            def level_arg(n):
                lv, d = n // 2, n % 2
                half = 2 ** lv
                if n >= 2:
                    v.wait_ge(S("lv_mm"), n - 1)
                left, right = level_views(LC[d], half)
                oleft, oright = level_views(EX[:, n % 2], half)
                at = left[:, :, half - 1:half] if d == 0 else right[:, :, 0:1]
                at = at.broadcast_to([P, 1024 // half, half])
                link(tt(oleft, at, left, ALU.subtract))
                link(tt(oright, right, at, ALU.subtract))
                v.sem_inc(S("lv_arg"), 1)

            def level_mul(n):
                lv, d = n // 2, n % 2
                half = 2 ** lv
                if n < 16:
                    v.wait_ge(S("lv_exp"), n + 1)
                    oleft, oright = level_views(EX[:, n % 2], half)
                    kl, kr = level_views((FF_, FB_)[d], half)
                    ql, qr = level_views(QH, half)
                    link(tt(oleft, oleft, kl if d == 0 else ql, ALU.mult))
                    link(tt(oright, oright, qr if d == 0 else kr, ALU.mult))
                else:
                    v.wait_ge(S("lv_mm"), n - 1)
                    link(tt(EX[:, 0], FF_, FB_, ALU.add))
                v.sem_inc(S("lv_x"), 1)

            def level_put(n):
                lv, d = n // 2, n % 2
                v.wait_ge(S("lv_mm"), n + 1)
                b0 = 4 * (n % 2)
                if lv == 7:
                    link(nc.vector.tensor_copy(SCO[:, d].rearrange("p h t -> p (h t)"), bank(b0, 2)))
                else:
                    m = 14 if n == 16 else 7 * d + lv
                    link(nc.vector.copy_predicated(SCD, MASKS[:, m, :].unsqueeze(1).broadcast_to([P, 16, P]),
                                                   bank(b0, 4).rearrange("p (x t) -> p x t", x=16)))
                v.sem_inc(S("lv_put"), 1)

            level_arg(0)
            for n in range(17):
                if n < 15:
                    level_arg(n + 1)
                level_mul(n)
                if n:
                    level_put(n - 1)
            level_put(16)
            link(nc.vector.memset(acc[:], 0.0))
            v.wait_ge(S("rms_std"), 2)
            link(nc.vector.reciprocal(RS, RS))
            link(stt(OB, OB, HGG, RS, ALU.mult, ALU.mult))
            link(tt(OB, OB, GH, ALU.mult))
            v.sem_inc(S("o_ready"), 1)
            for k, o in enumerate((Pb[:, 0:8, :], Pb[:, 32:40, :])):
                v.wait_ge(S("o_hi"), k + 1)
                link(tt(Hlo[:, 8 * k:8 * k + 8], o, Hhi[:, 8 * k:8 * k + 8].bitcast(F), ALU.subtract))
            v.sem_inc(S("h_ready"), 1)

            s = plan_out[0]

            def evac_out(blk):
                v.wait_ge(S("slab_used"), s.G + 4 * blk + 4 + PRIME_USED)
                for m in range(4):
                    kt = 4 * blk + m
                    ins = stt(X[:, kt], PS[:, 2 * (blk % 2) + m // 2, (m % 2) * T:(m % 2 + 1) * T],
                              G1[:, 0, kt:kt + 1], X[:, kt], ALU.mult, ALU.add)
                ins.then_inc(S("evac_done"), 1)
            v.wait_ge(S("x_scaled"), 1)
            for blk in range(4):
                for sl in range(4):
                    split_lo(v, blk, s.B, s.G, sl)
                    if sl == 1 and blk:
                        evac_out(blk - 1)
            evac_out(3)
            v.wait_ge(S("evac_done"), s.E + 4 + PRIME_EVAC)
            modulation(1, 0)
            layer_norm(0)
            make_h(1, 3)
            for layer in range(2):
                if layer == 1:
                    v.wait_ge(S("u_ready"), 256)
                    link(tt(YT, UT, Dsk[:].unsqueeze(2).broadcast_to([P, 64, 64]), ALU.mult))
                    v.wait_ge(S("sv_evac"), 16)
                    A4v = A4[:].rearrange("p (a c) x -> p a c x", a=2)
                    with v.Fori(1, 63) as k:
                        lk = stepper(v, "scan_steps", k - 1, 5)
                        old, new = SV[:, bass.ds(k - 1, 1)], SV[:, bass.ds(k, 1)]
                        old, new = (z.rearrange("p n c x -> p (n c) x") for z in (old, new))
                        lk(tt(STP[:, 0], A4v[:, 0], old, ALU.mult))
                        lk(tt(STP[:, 1, 0], A4v[:, 1, 0], old[:, 1], ALU.mult))
                        lk(tt(STP[:, 1, 1], A4v[:, 1, 1], old[:, 0], ALU.mult))
                        lk(tt(STP[:, 0], STP[:, 0], STP[:, 1], ALU.add))
                        lk(tt(new, new, STP[:, 0], ALU.add))
                    v.sem_inc(S("s5_scan"), 1)
                    for q in range(4):
                        v.wait_ge(S("mat_used"), 16 + 5 * (q + 1))
                        yq = HF[:, 1024 * q:1024 * q + 1024]
                        link(tt(yq, yq, bank(2 * q, 2), ALU.add))
                    v.sem_inc(S("ge_in"), 1)
                    v.wait_ge(S("ge_sq"), 1)
                    t_ = PF[:, 8192:12288]
                    link(ts(t_, t_, 0.044715, 1.0, ALU.mult, ALU.add))
                    link(tt(t_, t_, HF[:, 0:4096], ALU.mult))
                    v.sem_inc(S("ge_in"), 1)
                    v.wait_ge(S("ge_sig"), 1)
                    link(tt(HF[:, 0:4096], HF[:, 0:4096], t_, ALU.mult))
                    v.sem_inc(S("y_ready"), 1)
                    v.wait_ge(S("o_hi"), 3)
                    link(tt(Hlo[:].rearrange("p k t -> p (k t)"), PF[:, 0:4096],
                            Hhi[:].rearrange("p k t -> p (k t)").bitcast(F), ALU.subtract))
                    v.sem_inc(S("h_ready"), 1)
                    split_lows(plan_glu)
                    v.wait_ge(S("evac_done"), plan_glu[1].E + 4 + PRIME_EVAC)
                    v.wait_ge(S("x_scaled"), 3)
                    link(tt(PF[:, 4096:8192], PF[:, 4096:8192], PF[:, 8192:12288], ALU.mult))
                    for kt in range(KT):
                        xv = X[:, kt].rearrange("p (n j) -> p j n", j=4)
                        link(stt(xv, Pb[:, 16 + kt].rearrange("p (j n) -> p j n", j=4), G1[:, 2, kt:kt + 1], xv,
                                 ALU.mult, ALU.add))
                    modulation(3, 2)
                    layer_norm(2)
                    make_h(2, 5)
                up, dn = plan_mlp[layer]
                fin = split_lows(up)
                fin = split_lows(dn, fin=fin, down=2 * layer)
                evac_down(dn[1], 2 * layer)
                if fin:
                    ada_finish(v, link, fin.N, fin.ada[0], fin.ada[1], 0)
                if layer == 0:
                    modulation(2, 1)
                layer_norm(1 + 2 * layer)
                if layer == 0:
                    for kt in range(KT):
                        ins = ts(HS[:, kt].rearrange("p j n -> p n j"), X[:, kt].rearrange("p (n j) -> p n j", j=4),
                                 HA[:, 0, kt:kt + 1], HA[:, 1, kt:kt + 1], ALU.mult, ALU.add)
                    link(ins)
                    v.sem_inc(S("hs_ready"), 1)
            for kt in range(KT):
                ins = ts(X[:, kt], X[:, kt], LNG[3][:, kt:kt + 1], LNB[3][:, kt:kt + 1], ALU.mult, ALU.add)
            link(ins)
            v.sem_inc(S("x_final"), 1)

        @block.gpsimd
        def _(pool):
            pool.wait_ge(S("pw_ready"), 1)
            with pool.Fori(0, 16) as n:
                lk = stepper(pool, "p_steps", n, 8)
                pool.wait_ge(S("taps"), n + PRIME_MAT)
                pool.wait_ge(S("out_stored"), n * 64 + 16 * PRIME_MAT)
                pad(nc.gpsimd, lk, Op, TG, PWO, CTt, n * 8, 5, (0, 1, 2))
                pool.sem_inc(S("pad_ready"), 1)
            for k in range(4):
                pool.wait_ge(S("xab_ready"), k + 1)
                if k == 2:
                    pool.wait_ge(S("hs_ready"), 1)
                else:
                    pool.wait_ge(S("h32"), 4 * (k if k < 3 else 2) + 4)
                for kt in range(KT):
                    ins = nc.gpsimd.tensor_scalar(X[:, kt], X[:, kt], XAB[:, 0, kt:kt + 1], XAB[:, 1, kt:kt + 1],
                                                  ALU.mult, ALU.add)
                ins.then_inc(S("x_scaled"), 1)


NAMES = ["x", "c", "ada_w", "ada_b", "ln_g", "ln_b", "mix_w_in", "mix_w_out", "diff_lambda", "diff_subln_g",
         "hg_lower_bound", "hg_norm_g", "s5_lambda_re", "s5_lambda_im", "s5_log_dt", "s5_b_re", "s5_b_im",
         "s5_c_re", "s5_c_im", "s5_d", "s5_w_glu", "mlp_w1", "mlp_w2"]


def constants():
    ident = np.eye(P, dtype=np.float32)
    rot = np.zeros((P, P), np.float32)
    cos, sin = np.ones((P, T), np.float32), np.zeros((P, T), np.float32)
    inv = (1.0 / (np.float32(500000.0) ** (np.arange(0, 16, 2, dtype=np.float32) / np.float32(16)))).astype(np.float32)
    ang = (np.arange(T, dtype=np.float32)[:, None] * inv[None, :]).astype(np.float32).T
    for c in range(2):
        for r in range(8):
            lo, hi = 64 * c + r, 64 * c + 8 + r
            rot[hi, lo], rot[lo, hi] = -1.0, 1.0
            cos[lo] = cos[hi] = np.cos(ang[r])
            sin[lo] = sin[hi] = np.sin(ang[r])
    s, t = np.meshgrid(np.arange(P), np.arange(P), indexing="ij")
    masks = np.zeros((15, P, P), np.float32)
    for lv in range(7):
        apart = ((s >> lv) ^ (t >> lv)) == 1
        masks[lv], masks[7 + lv] = apart & (s < t), apart & (s > t)
    masks[14] = s == t
    return {"ident": ident, "rot": rot, "cos": cos, "sin": sin, "masks": masks}


def kernel(**inputs):
    import concourse.bacc as _bacc
    from concourse.bass_utils import run_bass_kernel_spmd as _run

    nc = _bacc.Bacc("TRN2", target_bir_lowering=False, num_devices=1)
    arrays, aps = {}, {}
    for name, arr in list((n, inputs[n]) for n in NAMES) + list(constants().items()):
        arr = np.ascontiguousarray(arr)
        arrays[f"in_{name}"] = arr
        aps[name] = nc.dram_tensor(f"in_{name}", arr.shape, mybir.dt.from_np(arr.dtype), kind="ExternalInput").ap()
    out = nc.dram_tensor("out_y", (1, T, D), F, kind="ExternalOutput").ap()
    trunk(nc, aps, out)
    r = _run(nc, [arrays], core_ids=[0])
    return r.results[0]["out_y"]
```

```python
import math

import numpy as np
import concourse.bass as bass
from concourse import mybir

F = mybir.dt.float32
R = mybir.dt.float32r
I32 = mybir.dt.int32
ALU = mybir.AluOpType
ACT = mybir.ActivationFunctionType
AX = mybir.AxisListType

P = 128
D = 2048
T = 256
KT = D // P
DFF = 4 * D
HEADS = 8
LEVELS = 8
SLAB = 2048
ALPHA = 4 ** 0.25
LN_EPS, RMS_EPS = 1e-5, 1e-6
LAM_INIT = 0.8 - 0.6 * math.exp(0.0)
QK_SCALE = 64 ** -0.5
C4 = 4
NCH = T // C4
TILES5 = 64
MAGIC = 1.5 * 2 ** 23
ADA_HALF = 1024
ADA_COLS = 3072
GELU_C = math.sqrt(2 / math.pi)
PRIME_RAW, PRIME_USED, PRIME_EVAC, PRIME_MAT, PRIME_TAPS, PRIME_GV = 4, 2, 2, 1, 2, 4


def trunk(nc, a, out):
    sems = {}

    def S(name):
        if name not in sems:
            sems[name] = nc.alloc_semaphore(name)
        return sems[name]

    X = nc.alloc_sbuf_tensor("X", [P, KT, T], F)
    h_base = nc.sbuf_base
    Hhi = nc.alloc_sbuf_tensor("Hhi", [P, KT, T], R)
    Hlo = nc.alloc_sbuf_tensor("Hlo", [P, KT, T], R)
    HF = nc.alloc_sbuf_tensor_at("HF", [P, 8192], F, offset=h_base)
    Pb = nc.alloc_sbuf_tensor("Pb", [P, 64, T], F)
    PF = Pb[:].rearrange("p a t -> p (a t)")
    raw = nc.alloc_sbuf_tensor("raw", [P, 4, SLAB], F)
    w_base = nc.sbuf_base
    whi = nc.alloc_sbuf_tensor("whi", [P, 2, SLAB], R)
    wlo = nc.alloc_sbuf_tensor("wlo", [P, 2, SLAB], R)
    WF = nc.alloc_sbuf_tensor_at("WF", [P, 8192], F, offset=w_base)
    acc = nc.alloc_sbuf_tensor("acc", [P, ADA_COLS], F)
    araw = nc.alloc_sbuf_tensor("araw", [P, 3, ADA_HALF], F)
    ident = nc.alloc_sbuf_tensor("ident", [P, P], F)
    ones = nc.alloc_sbuf_tensor("ones", [P, T], F)
    PT = nc.alloc_sbuf_tensor("PT", [P, 4, P], F)
    MOD = nc.alloc_sbuf_tensor("MOD", [P, 4, 48], F)
    HA = nc.alloc_sbuf_tensor("HA", [P, 2, KT], F)
    G1 = nc.alloc_sbuf_tensor("G1", [P, 4, KT], F)
    cact = nc.alloc_sbuf_tensor("cact", [P, KT], F)
    small = nc.alloc_sbuf_tensor("small", [P, 64], F)
    CW = nc.alloc_sbuf_tensor("CW", [P, 4, 23], F)
    lbs = nc.alloc_sbuf_tensor("lbs", [P, 2, 16], F)
    lamb = nc.alloc_sbuf_tensor("lamb", [P, 2], F)
    eps = nc.alloc_sbuf_tensor("eps", [P, 2], F)
    A4 = nc.alloc_sbuf_tensor("A4", [P, 4, P], F)
    Dsk = nc.alloc_sbuf_tensor("Dsk", [P, TILES5], F)
    PS = nc.alloc_psum_tensor("PS", [P, 8, 512], F)
    vmat = nc.dram_tensor("vmat", [16, P, SLAB], F, kind="Internal").ap()
    omat = nc.dram_tensor("omat", [20, P, SLAB], F, kind="Internal").ap()

    ZERO2 = small[:, 62:64]
    ADAB = [PT[:, i // 2, 48 * (i % 2):48 * (i % 2) + 48] for i in range(4)]
    LNG = [PT[:, 2, 16 * i:16 * i + 16] for i in range(4)]
    LNB = [PT[:, 2, 64 + 16 * i:80 + 16 * i] for i in range(4)]
    CRAW, LBR = PT[:, 3, 0:16], PT[:, 3, 16:64]
    SUBG, HGG = PT[:, 3, 64:65], PT[:, 3, 65:66]

    def bank(b, n=1):
        return PS[:, b:b + n, :].rearrange("p b c -> p (b c)")

    def settle(eng):
        eng.sem_inc(S("settled"), 1)

    def chain(eng, name):
        count = [0]

        def link(ins):
            count[0] += 1
            ins.then_inc(S(name), 1)
            eng.wait_ge(S(name), count[0])
        return link

    STG = WF[:, 0:512].rearrange("p (a c) -> p a c", a=4)
    LS = WF[:, 512:1280].rearrange("p (a c) -> p a c", a=6)
    LDT = WF[:, 1280:1284].rearrange("p (a c) -> p a c", a=2)
    DST = WF[:, 1536:1664].rearrange("p (a c) -> p a c", a=4)
    LAMR = WF[:, 1664:1920].rearrange("p (a c) -> p a c", a=4)
    LTMP = WF[:, 1920:2048].rearrange("p (a c) -> p a c", a=2)
    VS = WF[:, 2048:4096].rearrange("p (d c t m) -> p d c t m", d=2, c=2, t=4)
    RAWF = raw[:].rearrange("p a m -> p (a m)")
    O_AREAS = [WF[:, 4096:6656], RAWF[:, 0:2560]]
    V_AREAS = [PF[:, 4096:6144], RAWF[:, 2560:4608]]
    R_AREAS = [WF[:, 0:2048], RAWF[:, 4608:6656]]
    Op = [z.rearrange("p (c t s m) -> p c t s m", c=2, t=8, s=5) for z in O_AREAS]
    TP = WF[:, 6656:7936].rearrange("p (a x) -> p a x", a=2)
    Vp = [z.rearrange("p (c t s m) -> p c t s m", c=2, t=8, s=4) for z in V_AREAS]
    INTRA = PF[:, 0:2048].rearrange("p (t m) -> p t m", t=16)
    TG = PF[:, 2048:3328].rearrange("p (a x) -> p a x", a=2)
    Bn = PF[:, 6144:10240].rearrange("p (c x h) -> p c x h", c=2, h=16)
    Cn = PF[:, 10240:14336].rearrange("p (a t x) -> p a t x", a=4, t=8)
    CTt = HF[:, 0:4096].rearrange("p (c x h) -> p c x h", c=2, h=16)
    BB = HF[:, 4096:8192].rearrange("p (c x h) -> p c x h", c=2, h=16)
    PW = PF[:, 14336:15360].rearrange("p (k c x) -> p k c x", k=4, c=2)
    TM = PF[:, 15360:16384].rearrange("p (a x) -> p a x", a=8)
    PWV = PF[:, 10240:11264].rearrange("p (c x s) -> p c x s", c=2, s=4)
    PWO = PF[:, 11264:13184].rearrange("p (c x s) -> p c x s", c=3, s=5)
    XN = PF[:, 0:4096].rearrange("p (a d) -> p a d", a=2)

    ada_w = a["ada_w"].rearrange("l s k m -> (l s k) m")

    ADA = [(0, 2 * D, 2), (2, 0, 3), (2, ADA_COLS, 3), (3, 2 * D, 2)]

    def ada_loads(sp, i, u, k0):
        sub, col, halves = ADA[u]
        for r in range(halves):
            sp.wait_ge(S(f"ada{u}_used"), i * halves + (k0 * halves + r + 1))
            row = (i + (sub * KT + k0)) * P
            sp.dma_start(araw[:, r, :], ada_w[bass.ds(row, P), col + r * ADA_HALF:col + (r + 1) * ADA_HALF]
                         ).then_inc(S(f"ada{u}_ready{r}"), 16)

    def ada_mac(v, i, u, k0, r):
        halves = ADA[u][2]
        v.wait_ge(S(f"ada{u}_ready{r}"), i * 16 + (k0 + 1) * 16)
        v.wait_ge(S(f"ada{u}_used"), i * halves + (k0 * halves + r + 1))
        cols = acc[:, r * ADA_HALF:(r + 1) * ADA_HALF]
        nc.vector.scalar_tensor_tensor(out=cols, in0=araw[:, r, :],
                                       scalar=cact[:, bass.ds(i + k0, 1)], in1=cols,
                                       op0=ALU.mult, op1=ALU.add).then_inc(S(f"ada{u}_used"), 1)

    def ada_sum_pe(pe, u, b):
        halves = ADA[u][2]
        pe.wait_ge(S(f"ada{u}_used"), (KT + 1) * halves)
        for m in range(8 * halves):
            last = nc.tensor.matmul(PS[:, b, m:m + 1], acc[:, m * P:(m + 1) * P], ones[:, 0:1],
                                    start=True, stop=True)
        last.then_inc(S(f"ada{u}_summed"), 1)

    def ada_finish(v, link, u, b):
        sub, col, halves = ADA[u]
        v.wait_ge(S(f"ada{u}_summed"), 1)
        ms = slice(col // P, col // P + 8 * halves)
        link(nc.vector.tensor_tensor(MOD[:, sub, ms], PS[:, b, 0:8 * halves], ADAB[sub][:, ms], ALU.add))
        if u in (0, 3):
            link(nc.vector.tensor_scalar(G1[:, sub], MOD[:, sub, 32:48], 1.0, None, ALU.add))
        else:
            link(nc.vector.memset(acc[:], 0.0))
        v.sem_inc(S("ada_freed"), 1)

    accf, arawf = acc[:], araw[:].rearrange("p a c -> p (a c)")
    GV = {0: (0, 7, [accf[:, 0:1024], accf[:, 1024:2048], arawf[:, 0:1024], arawf[:, 1024:2048]]),
          1: (1, 7, None),
          2: (3, 7, [WF[:, 1024 * p:1024 * (p + 1)] for p in range(4)])}
    PART_ROWS = 2
    ROWS = 3 * D // 512
    PACC = WF[:, 0:3 * D]
    GT = acc[0:ROWS, 2560:3072]

    def gemv_loads(sp, n, k):
        sub, _, areas = GV[n]
        for p in range(4):
            sp.wait_ge(S(f"gv{n}_used"), k * 4 + (p + 1))
            row = k * P + sub * D
            cols = PART_ROWS * 512
            sp.dma_start(areas[p], ada_w[bass.ds(row, P), p * cols:(p + 1) * cols]
                         ).then_inc(S(f"gv{n}_ready{p}"), 16)

    def gemv_open(n):
        nc.tensor.matmul(PS[:, GV[n][1], 0:2], ones[:, 0:P], ZERO2, start=True, stop=True, skip_group_check=True)

    def gemv_row(n, w, r, src):
        return nc.tensor.matmul(PS[0:ROWS, GV[n][1], :], CW[:, w, ROWS - 1 - r:2 * ROWS - 1 - r], src,
                                start=False, stop=True, skip_group_check=True)

    def gemv_part(pe, n, k, p, w):
        pe.wait_ge(S(f"gv{n}_ready{p}"), k * 16 + 16)
        for x in range(PART_ROWS):
            last = gemv_row(n, w, PART_ROWS * p + x, GV[n][2][p][:, x * 512:(x + 1) * 512])
        last.then_inc(S(f"gv{n}_used"), 1)

    def gemv_window(act, k, w):
        nc.scalar.activation(CW[:, w, ROWS - 1:ROWS], cact[:, bass.ds(k, 1)], ACT.Copy).then_inc(S("cw_ready"), 1)

    def gemv_turn(pe, n):
        pe.wait_ge(S("gv_copied"), n + 1)
        for x in range(4):
            last = nc.tensor.transpose(PS[:, GV[n][1], x * ROWS:(x + 1) * ROWS], GT[:, x * P:(x + 1) * P],
                                       ident[0:ROWS, 0:ROWS])
        last.then_inc(S("gv_T"), 1)

    def gemv_copy(v, link, n, sem, count):
        v.wait_ge(S(sem), count)
        link(nc.vector.tensor_copy(GT, PS[0:ROWS, GV[n][1], :]))
        v.sem_inc(S("gv_copied"), 1)

    def gemv_finish(v, link, n):
        sub, b, _ = GV[n]
        v.wait_ge(S("gv_T"), n + 1)
        mod, bias = (z.rearrange("p (r x) -> p x r", x=4) for z in (MOD[:, sub], ADAB[sub]))
        link(nc.vector.tensor_tensor(mod, PS[:, b, 0:48].rearrange("p (x r) -> p x r", x=4), bias, ALU.add))
        v.sem_inc(S("gv_freed"), 1)

    def slab_loads(sp, i, B, G, src):
        for s in range(4):
            sp.wait_ge(S("lo_done"), i * 4 + (G + s + 1))
            sp.dma_start(raw[:, s, :], src(i, s)).then_inc(S(f"raw_ready{s}"), 16)

    def split_hi(act, i, B, G, s):
        act.wait_ge(S(f"raw_ready{s}"), i * 16 + (B + 1) * 16)
        act.wait_ge(S("slab_used"), i * 4 + (G + s + 1))
        nc.scalar.activation(whi[:, s % 2, :], raw[:, s, :], ACT.Copy).then_inc(S("hi_done"), 1)

    def split_lo(v, i, B, G, s):
        v.wait_ge(S("hi_done"), i * 4 + (G + s + 1))
        nc.vector.tensor_tensor(wlo[:, s % 2, :], raw[:, s, :], whi[:, s % 2, :].bitcast(F),
                                ALU.subtract).then_inc(S("lo_done"), 1)

    def three(ps, w, xh, xl, first, last):
        nc.tensor.matmul(ps, w[0], xh, start=first, stop=False, skip_group_check=True)
        nc.tensor.matmul(ps, w[0], xl, start=False, stop=False, skip_group_check=True)
        return nc.tensor.matmul(ps, w[1], xh, start=False, stop=last, skip_group_check=True)

    def block_products(pe, evacs, slabs, par, h=None):
        pe.wait_ge(S("evac_done"), evacs)
        for s in range(4):
            pe.wait_ge(S("lo_done"), slabs + s)
            if h is not None:
                pe.wait_ge(S("h_ready"), 4 * h + s + 1)
            for kt in range(4):
                k = 4 * s + kt
                for m in range(4):
                    at = slice(kt * 512 + m * P, kt * 512 + (m + 1) * P)
                    last = three(PS[:, 2 * par + m // 2, (m % 2) * T:(m % 2 + 1) * T],
                                 (whi[:, s % 2, at], wlo[:, s % 2, at]), Hhi[:, k, :], Hlo[:, k, :],
                                 first=(k == 0 and m % 2 == 0), last=(k == KT - 1))
            last.then_inc(S("slab_used"), 1)

    class Seg:
        pass
    plan = []
    cB = cG = cE = 0

    def seg(name, bodies, src, split=True, ada=None, evacs=0, half=0):
        nonlocal cB, cG, cE
        s = Seg()
        s.name, s.bodies, s.src, s.split, s.ada = name, bodies, src, split, ada
        s.B, s.G, s.E = cB, cG, cE
        s.half = half
        cB += bodies
        cG += 4 * bodies * split
        cE += evacs
        plan.append(s)
        return s

    def rows(w, n0=0):
        def src(i, s):
            return w[4 * s * P:(4 * s + 4) * P, bass.ds((i + n0) * 512, 512)].rearrange(
                "(a p) m -> p a m", p=P)
        return src

    def down(w, half):
        def src(i, s):
            return w[bass.ds((i * 8 + 2 * s) * P, 2 * P), half * 1024:(half + 1) * 1024].rearrange(
                "(a p) m -> p a m", p=P)
        return src

    w_in, w_out, w_glu = a["mix_w_in"][0], a["mix_w_out"][0], a["s5_w_glu"][0]
    plan_in = [seg("block", 8, rows(w_in, 8 * c), evacs=8, ada=(0, 8 * c)) for c in range(2)]
    plan_out = [seg("block", 4, rows(w_out), evacs=4)]
    plan_mlp = []
    for layer in range(2):
        if layer == 1:
            plan_v = seg("mats", 4, lambda i, s: vmat[bass.ds(i * 4 + s, 1)].rearrange("o p m -> p (o m)"),
                         split=False)
            plan_o = seg("mats", 5, lambda i, s: omat[bass.ds(i * 4 + s, 1)].rearrange("o p m -> p (o m)"),
                         split=False)
            plan_glu = [seg("block", 4, rows(w_glu, 4 * c), evacs=4) for c in range(2)]
        up = [seg("block", 8, rows(a["mlp_w1"][layer], 8 * c), evacs=8,
                  ada=(3 if layer else 1, 8 * c)) for c in range(2)]
        dn = [seg("down", 8, down(a["mlp_w2"][layer], h), half=h,
                  ada=None if layer else (2, 8 * h)) for h in range(2)]
        plan_mlp.append((up, dn))
    GALL = cG


    ROTW = acc[:, 0:128]
    COS = acc[:, 128:384]
    SIN = acc[:, 384:640]
    MASKS = acc[:, 640:2560].bitcast(I32).rearrange("p (m t) -> p m t", m=15)
    ROTT = HF[:, 4096:4608].rearrange("p (b t) -> p b t", b=2)
    Vn = HF[:, 0:2048].rearrange("p (h a e) -> p h a e", h=8, a=2)
    EA = HF[:, 2048:3072].rearrange("p (b c t) -> p b c t", b=2, c=2)
    AT = HF[:, 3072:3584].rearrange("p (b a t) -> p b a t", b=2, a=2)
    VH = PF[:, 4096:6144].rearrange("p (h a e) -> p h a e", h=8, a=2)
    LC = [PF[:, 2048:4096], PF[:, 12288:14336]]
    SCO = HF[:, 6144:8192].rearrange("p (d h t) -> p d h t", d=2, h=8)
    SCDF = HF[:, 4096:6144]
    SCD = HF[:, 4096:6144].rearrange("p (x t) -> p x t", x=16)
    EX = [HF[:, 0:2048], HF[:, 2048:4096], WF[:, 6144:8192]]
    QH, FF_, FB_, IB_, GH = (PF[:, o * T:(o + 8) * T] for o in (24, 32, 40, 48, 56))
    OA, OB = PF[:, 0:2048], PF[:, 8192:10240]
    mx, nm, sm, rc = ([small[:, 32 + 4 * k + 2 * p:34 + 4 * k + 2 * p] for p in range(2)] for k in range(4))
    HS = HF[:, 0:4096].rearrange("p (k j n) -> p k j n", k=16, j=4)
    UT = HF[:, 4096:8192].rearrange("p (t n) -> p t n", t=64)
    YT = HF[:, 0:4096].rearrange("p (t n) -> p t n", t=64)
    GLF = WF[:, 4096:8192]
    GF = GLF.rearrange("p (k j n) -> p k j n", k=16, j=4)
    SV = PF[:, :].rearrange("p (n c x) -> p n c x", c=2, x=128)
    STP = acc[:, 0:512].rearrange("p (a c x) -> p a c x", a=2, c=2)
    ON = PF[:, 0:4096].rearrange("p (a d) -> p a d", a=2)
    XAB = small[:, 0:32].rearrange("p (a k) -> p a k", a=2)

    LNS = HF[:, 7936:8192]
    SQ, RS = HF[:, 0:2048], HF[:, 2048:4096]

    Rp = [z.rearrange("p (c x m) -> p c x m", c=2, x=8) for z in R_AREAS]
    LT = LTMP

    def pad(eng, lk, dst, tmps, pw, w, x, slots, signs):
        shape = [P, 8, slots, 16]
        pr, pi, q = (pw[:, k, bass.ds(x, 8), :].unsqueeze(3).broadcast_to(shape) for k in signs)
        wr, wi = (w[:, k, bass.ds(x, 8), :].unsqueeze(2).broadcast_to(shape) for k in range(2))
        t0, t1 = (tmps[:, k, 0:8 * slots * 16].rearrange("p (x s h) -> p x s h", s=slots, h=16)
                  for k in range(2))
        for c in range(2):
            settle(eng)
            lk(eng.tensor_tensor(t0, (pr, q)[c], (wr, wi)[c], ALU.mult))
            settle(eng)
            lk(eng.tensor_tensor(t1, pi, (wi, wr)[c], ALU.mult))
            for g in range(2):
                half = slice(64 * g, 64 * g + 64)
                lk(eng.tensor_tensor(dst[half, c, :, :, 16 * g:16 * g + 16], t0[half], t1[half],
                                     ALU.add if (c == 1 and slots == 4) else ALU.subtract))

    def stepper(eng, name, i, per):
        count = [0]

        def lk(ins):
            count[0] += 1
            ins.then_inc(S(name), 1)
            eng.wait_ge(S(name), i * per + count[0])
        return lk

    def rms_pe(pe, n, src):
        pe.wait_ge(S("cw_ready"), 17)
        pe.wait_ge(S("rms_sq"), n)
        for h in range(8):
            last = nc.tensor.matmul(PS[0:ROWS, 0, 0:T], CW[:, 3, ROWS - 1 - h:2 * ROWS - 1 - h],
                                    src[:, h * T:(h + 1) * T], start=(h == 0), stop=(h == 7))
        last.then_inc(S("rms_sum"), 1)
        pe.wait_ge(S("rms_inv"), n)
        for h in range(8):
            last = nc.tensor.matmul(PS[:, h // 2, (h % 2) * T:(h % 2 + 1) * T],
                                    ident[0:ROWS, h:h + 1].broadcast_to([ROWS, P]), RS[0:ROWS, 0:T],
                                    start=True, stop=True)
        last.then_inc(S("rms_wide"), 1)

    with nc.Block() as block:
        @block.sync
        def _(sp):
            def load(dst, src, sem):
                sp.dma_start(dst, src).then_inc(S(sem), 16)

            for name in ("v_stored", "intra_stored"):
                sp.sem_inc(S(name), 16 * PRIME_MAT)
            for par in range(2):
                sp.sem_inc(S(f"out_stored{par}"), 64 * PRIME_MAT)
            sp.wait_ge(S("stg_zero"), 1)
            load(ident[:], a["ident"], "ld_const")
            load(STG[0:96, 0, :], a["ada_b"].rearrange("l s (m p) -> (l s m) p", p=P)[0:96], "ld_par")
            load(STG[0:96, 1, :], a["ada_b"].rearrange("l s (m p) -> (l s m) p", p=P)[96:192], "ld_par")
            load(STG[0:64, 2, :], a["ln_g"].rearrange("l s (m p) -> (l s m) p", p=P), "ld_par")
            load(STG[64:128, 2, :], a["ln_b"].rearrange("l s (m p) -> (l s m) p", p=P), "ld_par")
            load(STG[0:16, 3, :], a["c"].rearrange("b (m p) -> (b m) p", p=P), "ld_par")
            load(STG[16:64, 3, :], a["hg_lower_bound"].rearrange("d l (m p) -> (d l m) p", p=P), "ld_par")
            load(STG[64:65, 3, :], a["diff_subln_g"], "ld_par")
            load(STG[65:66, 3, :], a["hg_norm_g"], "ld_par")
            load(LAMR, a["diff_lambda"][0].partition_broadcast(P), "ld_par")
            for d in range(2):
                load(LS[0:64, d, :], a["s5_lambda_re"][0, d].rearrange("(t g) p -> t (g p)", g=2), "ld_s5")
                load(LS[0:64, 2 + d, :], a["s5_lambda_im"][0, d].rearrange("(t g) p -> t (g p)", g=2), "ld_s5")
                load(LDT[0:64, d, :], a["s5_log_dt"][0, d].rearrange("(t g) -> t g", g=2), "ld_s5")
            for j in range(4):
                load(DST[0:64, j, :], a["s5_d"][0].rearrange("(t c) -> t c", c=32), "ld_s5")
            load(XN, a["x"][0].rearrange("(a p) d -> p a d", p=P), "ld_x")
            for c, (bn, cn) in enumerate((("s5_b_re", "s5_c_re"), ("s5_b_im", "s5_c_im"))):
                for d in range(2):
                    bd = Bn[:, c].rearrange("p (k d t) h -> p d t k h", d=2, t=4)[:, d]
                    src = a[bn][0, d].rearrange("(k t g) p h -> t (g p) k h", g=2, t=4)
                    for t in range(4):
                        load(bd[:, t], src[t], "ld_b")
                    src = a[cn][0, d].rearrange("(T k g) h p -> k g h T p", g=2, k=8)
                    for k in range(8):
                        for g in range(2):
                            load(Cn[16 * k:16 * k + 16, 2 * d + c, :, 64 * g:64 * g + 64], src[k, g], "ld_c")
            sp.wait_ge(S("ones_ready"), 1)
            with sp.Fori(0, KT) as k:
                gemv_loads(sp, 0, k)
            sp.wait_ge(S("gv0_used"), 64 + PRIME_GV)
            sp.wait_ge(S("out_stored1"), 64 * (8 + PRIME_MAT))
            sp.wait_ge(S("taps"), 16 + PRIME_TAPS)

            def stream(s):
                if s.ada == (1, 0):
                    sp.wait_ge(S("pool_used"), 96 + 3)
                if s.ada in ((2, 0), (3, 0)):
                    sp.wait_ge(S(f"ada{s.ada[0] - 1}_used"), (KT + 1) * 3)
                with sp.Fori(0, s.bodies) as i:
                    slab_loads(sp, i, s.B, s.G, s.src)
                    if s.ada:
                        ada_loads(sp, i, *s.ada)

            for s in plan_in:
                stream(s)
            sp.wait_ge(S("in_done"), 1)
            sp.wait_ge(S("ada_freed"), 1)
            load(ROTW, a["rot"], "ld_rot")
            load(COS, a["cos"], "ld_rot")
            load(SIN, a["sin"], "ld_rot")
            load(acc[:, 640:2560].rearrange("p (m t) -> p m t", m=15), a["masks"].rearrange("m s t -> s m t"), "ld_rot")
            with sp.Fori(0, KT) as k:
                for r in range(6):
                    sp.wait_ge(S("pool_used"), k * 6 + (r + 1))
                    sp.dma_start(araw[:, r % 3, :], ada_w[bass.ds(k * P + D, P), r * ADA_HALF:(r + 1) * ADA_HALF]
                                 ).then_inc(S(f"pool_ready{r % 3}"), 16)
            for s in plan_out:
                stream(s)
            for layer in range(2):
                if layer == 1:
                    sp.wait_ge(S("v_stored"), 256 + 16 * PRIME_MAT)
                    for par in range(2):
                        sp.wait_ge(S(f"out_stored{par}"), 64 * (8 + PRIME_MAT))
                    sp.wait_ge(S("intra_stored"), 64 + 16 * PRIME_MAT)

                    def load_matrices(n):
                        if n < 4:
                            sp.wait_ge(S("lo_done"), plan_v.G + n + 1)
                        else:
                            sp.wait_ge(S("mat_used"), n - 3)
                        sp.dma_start(raw[:, n % 4, :], vmat[n] if n < 16 else omat[n - 16]
                                     ).then_inc(S(f"raw_ready{n % 4}"), 16)

                    def channels_back(g):
                        sp.wait_ge(S("y_ready"), g + 1)
                        for j in range(4):
                            for q in range(4):
                                sp.dma_start(
                                    GF[32 * q:32 * q + 32, 4 * g:4 * g + 4, j, :],
                                    YT[32 * j:32 * j + 32].rearrange("p (k a) n -> p a k n", a=4)[
                                        :, q, 4 * g:4 * g + 4]).then_inc(S(f"g_ready{g}"), 16)

                    for n in range(4):
                        load_matrices(n)
                    for half in range(2):
                        sp.wait_ge(S("hs_ready"), half + 1)
                        ks = slice(8 * half, 8 * half + 8)
                        for j in range(4):
                            for q in range(4):
                                sp.dma_start(
                                    UT[32 * j:32 * j + 32].rearrange("p (k a) n -> p a k n", a=4)[:, q, ks],
                                    HS[32 * q:32 * q + 32, ks, j, :]).then_inc(S(f"u_ready{half}"), 16)
                    for n in range(4, 36):
                        if n == 21:
                            with sp.Fori(0, KT) as k:
                                gemv_loads(sp, 2, k)
                        load_matrices(n)
                        if n in (24, 29, 34):
                            channels_back((24, 29, 34).index(n))
                    sp.wait_ge(S("mat_used"), 36)
                    first = plan_glu[0]
                    slab_loads(sp, 0, first.B, first.G, first.src)
                    channels_back(3)
                    with sp.Fori(1, first.bodies) as i:
                        slab_loads(sp, i, first.B, first.G, first.src)
                    stream(plan_glu[1])
                up, dn = plan_mlp[layer]
                for s in up + dn:
                    stream(s)
            for t in range(2):
                sp.wait_ge(S("out_ready"), t + 1)
                sp.dma_start(out[0].rearrange("(a p) d -> p a d", p=P)[:, t, :],
                             ON[:, t, :]).then_inc(S("stored"), 16)
            sp.wait_ge(S("stored"), 32)

        @block.tensor
        def _(pe):
            pe.sem_inc(S("slab_used"), PRIME_USED)
            pe.sem_inc(S("taps"), PRIME_TAPS)
            for n in (0, 2):
                pe.sem_inc(S(f"gv{n}_used"), PRIME_GV)
            pe.wait_ge(S("ld_const"), 16)
            pe.wait_ge(S("ld_par"), 9 * 16)
            pe.wait_ge(S("ones_ready"), 1)
            for t in range(4):
                last = nc.tensor.transpose(PS[:, 6, t * P:(t + 1) * P], STG[:, t, :], ident[:])
            last.then_inc(S("par_T"), 1)
            pe.wait_ge(S("ld_x"), 16)
            for kt in range(KT):
                if kt % 2 == 0 and kt >= 8:
                    pe.wait_ge(S("x_evac"), kt // 2 - 3)
                for t in range(2):
                    o = (kt % 2) * T + t * P
                    last = nc.tensor.transpose(PS[:, (kt // 2) % 4, o:o + P],
                                               XN[:, t, kt * P:(kt + 1) * P], ident[:])
                if kt % 2:
                    last.then_inc(S("x_T"), 1)
            pe.wait_ge(S("ls_ready"), 1)
            for t in range(6):
                nc.tensor.transpose(PS[:, 5, t * 64:(t + 1) * 64], LS[0:64, t, :], ident[0:64, 0:64])
            nc.tensor.transpose(PS[:, 5, 384:448], DST[0:64].rearrange("p a c -> p (a c)"), ident[0:64, 0:64]
                                ).then_inc(S("ls_T"), 1)
            pe.wait_ge(S("ld_c"), 64 * 16)
            pe.wait_ge(S("x_evac"), 8)
            for n in range(8):
                if n >= 4:
                    pe.wait_ge(S("c_evac"), n - 3)
                for t in range(4):
                    last = nc.tensor.transpose(PS[:, n % 4, t * P:(t + 1) * P], Cn[:, n // 2, 4 * (n % 2) + t, :],
                                               ident[:])
                last.then_inc(S("c_T"), 1)
            pe.wait_ge(S("c_evac"), 8)
            pe.wait_ge(S("ls_evac"), 1)
            pe.wait_ge(S("cw_ready"), 4)
            gemv_open(0)
            for k in range(4):
                for p in range(4):
                    gemv_part(pe, 0, k, p, k)
            with pe.Fori(0, 4) as q:
                for j in range(4):
                    par = j % 2
                    pe.wait_ge(S("vpad_ready"), q * 4 + (j + 1))
                    pe.wait_ge(S("vs_ready"), q * 4 + (j + PRIME_MAT))
                    for d in range(2):
                        for c in range(2):
                            for t in range(4):
                                last = nc.tensor.transpose(
                                    PS[:, 2 * d + c, t * P:(t + 1) * P],
                                    Vp[par][:, c, 4 * d + t].rearrange("p s m -> p (s m)"), ident[:])
                    last.then_inc(S("v_T"), 1)
                    pe.wait_ge(S("intra_ready"), q * 4 + (j + PRIME_MAT))
                    pe.wait_ge(S("opad_ready"), q * 4 + (j + 1))
                    pe.wait_ge(S("rp_ready"), q * 4 + (j + 1))
                    for d in range(2):
                        for t in range(4):
                            for c in range(2):
                                last = nc.tensor.matmul(
                                    PS[:, 4 + d, t * P:(t + 1) * P], Rp[par][:, c, 4 * d + t, :],
                                    Op[par][:, c, 4 * d + t, d:d + 4, :].rearrange("p s m -> p (s m)"),
                                    start=(c == 0), stop=(c == 1))
                    last.then_inc(S("taps"), 1)
                    pe.wait_ge(S("cw_ready"), q * 3 + (4 + 3))
                    for x in range(3 * j, 3 * j + 3):
                        gemv_part(pe, 0, q * 3 + (4 + x // 4), x % 4, x // 4)
            gemv_turn(pe, 0)

            def run_block(s, h=None):
                with pe.Fori(0, s.bodies // 2) as i:
                    for par in range(2):
                        block_products(pe, i * 2 + (s.E + par + 1), i * 8 + (s.G + 4 * par + 1 + PRIME_RAW), par,
                                       None if par else h)
                if s.ada and s.ada[1]:
                    ada_sum_pe(pe, s.ada[0], 4)

            def run_down(s, n):
                b0 = 4 * s.half
                if s.half:
                    pe.wait_ge(S("ada_freed"), n + 1)
                for b in range(b0, b0 + 4):
                    nc.tensor.matmul(PS[:, b, 0:2], ones[:, 0:P], ZERO2, start=True, stop=True,
                                     skip_group_check=True)
                with pe.Fori(0, 8) as i:
                    for sl in range(4):
                        pe.wait_ge(S("lo_done"), i * 4 + (s.G + sl + 1 + PRIME_RAW))
                        pe.wait_ge(S("hx_lo"), i * 4 + (n * 32 + sl + 1))
                        for kt in range(2):
                            k = 2 * (sl % 2) + kt
                            for m in range(8):
                                at = slice(kt * 1024 + m * P, kt * 1024 + (m + 1) * P)
                                last = three(PS[:, b0 + m // 2, (m % 2) * T:(m % 2 + 1) * T],
                                             (whi[:, sl % 2, at], wlo[:, sl % 2, at]),
                                             Hhi[:, k, :], Hlo[:, k, :], first=False, last=True)
                        last.then_inc(S("slab_used"), 1)
                if s.ada and s.half:
                    pe.wait_ge(S("down_evac"), n)
                    ada_sum_pe(pe, s.ada[0], 0)

            def layer_norm_pe(k):
                pe.wait_ge(S("ln_sum"), k + 1)
                nc.tensor.matmul(PS[:, 4, 0:T], ones[:, 0:P], LNS, start=True, stop=True).then_inc(S("ln_psum"), 1)
                for g in range(4):
                    pe.wait_ge(S("ln_sq"), 4 * k + g + 1)
                    for kt in range(4 * g, 4 * g + 4):
                        last = nc.tensor.matmul(PS[:, 5, 0:T], ones[:, 0:P], PF[:, kt * T:(kt + 1) * T],
                                                start=(kt == 0), stop=(kt == KT - 1))
                last.then_inc(S("ln_psum"), 1)

            def attention_pe():
                pe.wait_ge(S("in_done"), 1)
                for w in range(2):
                    for g in range(4):
                        if w == 1:
                            pe.wait_ge(S("vt_evac"), g + 1)
                        for x in range(4):
                            h, t = 2 * g + x // 2, x % 2
                            last = nc.tensor.transpose(PS[:, g, x * P:(x + 1) * P],
                                                       Pb[:, (16 if w == 0 else 48) + h, t * P:(t + 1) * P], ident[:])
                        last.then_inc(S("vt_T"), 1)
                pe.wait_ge(S("ld_rot"), 64)
                pe.wait_ge(S("ada_freed"), 1)
                for n in range(8):
                    if n >= 2:
                        pe.wait_ge(S("rot_done"), n - 1)
                    nc.tensor.matmul(PS[:, 4 + n % 2, :], ROTW, PF[:, n * 512:(n + 1) * 512], start=True, stop=True
                                     ).then_inc(S("rot_mm"), 1)
                pe.wait_ge(S("rot_done"), 8)
                pe.wait_ge(S("vt_evac"), 8)

                def scores(n):
                    h, qt = n // 2, n % 2
                    if n >= 2:
                        pe.wait_ge(S("at_exp"), n - 1)
                    for c in range(2):
                        last = nc.tensor.matmul(PS[:, 2 * (n % 2) + c, 0:T],
                                                Pb[64 * c:64 * c + 64, h, qt * P:(qt + 1) * P],
                                                Pb[64 * c:64 * c + 64, 8 + h, :], start=True, stop=True)
                    last.then_inc(S("at_score"), 1)

                for n in range(2):
                    scores(n)
                for n in range(16):
                    h, par = n // 2, n % 2
                    pe.wait_ge(S("at_mix"), n + 1)
                    for kt in range(2):
                        last = nc.tensor.transpose(PS[:, 4 + par, kt * P:(kt + 1) * P],
                                                   EA[:, par, 0, kt * P:(kt + 1) * P], ident[:])
                    last.then_inc(S("at_T"), 1)
                    if n < 14:
                        scores(n + 2)
                    pe.wait_ge(S("at_Te"), n + 1)
                    for kt in range(2):
                        last = nc.tensor.matmul(PS[:, 6 + par, 0:P], Vn[:, h, kt, :], AT[:, par, kt, :],
                                                start=(kt == 0), stop=(kt == 1))
                    last.then_inc(S("at_pv"), 1)
                rms_pe(pe, 1, SQ)

            def hgrn_pe():
                for n in range(17):
                    lv, d = n // 2, n % 2
                    b0 = 4 * (n % 2)
                    pe.wait_ge(S("lv_x"), n + 1)
                    if n >= 2:
                        pe.wait_ge(S("lv_put"), n - 1)
                    e = EX[n % 3].rearrange("p (h t) -> p h t", h=8)
                    for h in range(8):
                        for t in range(2):
                            x = e[:, h, t * P:(t + 1) * P]
                            if lv == 7 and t == 0:
                                y = e[:, h, P:2 * P]
                                last = nc.tensor.matmul(PS[:, b0 + h // 4, (h % 4) * P:(h % 4 + 1) * P],
                                                        x if d == 0 else y, y if d == 0 else x, start=True, stop=True)
                            elif lv != 7:
                                y = x if lv < 8 else QH.rearrange("p (h t) -> p h t", h=8)[:, h, t * P:(t + 1) * P]
                                z = 2 * h + t
                                last = nc.tensor.matmul(PS[:, b0 + z // 4, (z % 4) * P:(z % 4 + 1) * P],
                                                        x, y, start=True, stop=True)
                    last.then_inc(S("lv_mm"), 1)
                pe.wait_ge(S("lv_put"), 17)
                for h in range(8):
                    for t in range(2):
                        ps = PS[:, 4 + h // 2, (h % 2) * T + t * P:(h % 2) * T + (t + 1) * P]
                        nc.tensor.matmul(ps, VH[:, h, t], SCD[:, 2 * h + t], start=True, stop=False)
                        last = nc.tensor.matmul(ps, VH[:, h, 1 - t], SCO[:, 1 - t, h], start=False, stop=True)
                last.then_inc(S("hg_pv"), 1)
                rms_pe(pe, 2, SQ)
                pe.wait_ge(S("pool_used"), 96 + 3)
                gemv_open(1)
                for r in range(ROWS):
                    last = gemv_row(1, 3, r, PACC[:, r * 512:(r + 1) * 512])
                last.then_inc(S("pool_summed"), 1)
                gemv_turn(pe, 1)

            def s5_pe():
                B = plan_v.B
                for n in range(36):
                    if n in (0, 8):
                        pe.wait_ge(S(f"u_ready{n // 8}"), 256)
                    pe.wait_ge(S(f"raw_ready{n % 4}"), (B + n // 4 + 1) * 16)
                    mats = raw[:, n % 4, :].rearrange("p (x m) -> p x m", x=16)
                    if n < 16:
                        if n >= 4:
                            pe.wait_ge(S("sv_evac"), n - 3)
                        for d in range(2):
                            for c in range(2):
                                for t in range(4):
                                    o = d * 4 + t
                                    u = UT[:, 4 * n + t, :] if d == 0 else UT[:, 4 * n + t, ::-1]
                                    last = nc.tensor.matmul(
                                        PS[:, 2 * (n % 4) + c, o * 64:(o + 1) * 64],
                                        mats[:, 8 * d + 4 * c + t], u, start=True, stop=True)
                    else:
                        q, j = (n - 16) // 5, (n - 16) % 5
                        if j == 0:
                            if q == 0:
                                pe.wait_ge(S("sv_evac"), 16)
                            if q == 3:
                                pe.wait_ge(S("gv_freed"), 3)
                            for t in range(16):
                                last = nc.tensor.matmul(PS[:, 2 * q + t // 8, (t % 8) * 64:(t % 8 + 1) * 64],
                                                        mats[:, t], UT[:, 16 * q + t, :], start=(t % 8 == 0),
                                                        stop=False, skip_group_check=True)
                        else:
                            if n == 17:
                                gemv_open(2)
                                with pe.Fori(0, KT // 2) as kk:
                                    for w in range(2):
                                        pe.wait_ge(S("cw_ready"), kk * 2 + (w + 1 + 17))
                                        for p in range(4):
                                            gemv_part(pe, 2, kk * 2 + w, p, w)
                                gemv_turn(pe, 2)
                            pe.wait_ge(S("s5_scan"), 1)
                            for d in range(2):
                                for c in range(2):
                                    for t in range(4):
                                        tt = 4 * (j - 1) + t
                                        x = 8 * (4 * q + j - 1) + 4 * d + t
                                        st = SV[:, 0:63, c, x] if d == 0 else SV[:, 62::-1, c, x]
                                        o = (tt % 8) * 64 + (1 - d)
                                        last = nc.tensor.matmul(PS[:, 2 * q + tt // 8, o:o + 63],
                                                                mats[:, 8 * d + 4 * c + t], st, start=False,
                                                                stop=True, skip_group_check=True)
                    last.then_inc(S("mat_used"), 1)

            for n, s in enumerate(plan_in):
                run_block(s, 0 if n == 0 else None)
            attention_pe()
            hgrn_pe()
            for s in plan_out:
                run_block(s, 1)
            layer_norm_pe(0)
            for layer in range(2):
                if layer == 1:
                    s5_pe()
                    for n, s in enumerate(plan_glu):
                        run_block(s, 3 if n == 0 else None)
                    layer_norm_pe(2)
                up, dn = plan_mlp[layer]
                for n, s in enumerate(up):
                    run_block(s, (2 if layer == 0 else 4) if n == 0 else None)
                pe.wait_ge(S("evac_done"), up[1].E + 8 + PRIME_EVAC)
                for s in dn:
                    run_down(s, 2 * layer + s.half)
                layer_norm_pe(1 + 2 * layer)
            pe.wait_ge(S("x_final"), 1)
            for t in range(2):
                for g in range(4):
                    for x in range(4):
                        kt = 4 * g + x
                        last = nc.tensor.transpose(PS[:, 4 * t + g, x * P:(x + 1) * P],
                                                   X[:, kt, t * P:(t + 1) * P], ident[:])
                    last.then_inc(S("o_T"), 1)

        @block.scalar
        def _(act):
            link = chain(act, "act_chain")
            act.sem_inc(S("evac_done"), PRIME_EVAC)
            act.sem_inc(S("vs_ready"), PRIME_MAT)

            def run(out_, in_, func=ACT.Copy, sem=None, **kw):
                ins = nc.scalar.activation(out_, in_, func, **kw)
                if sem:
                    ins.then_inc(S(sem), 1)
                return ins

            act.wait_ge(S("par_ready"), 1)
            run(cact[:], CRAW, ACT.Sigmoid)
            run(TP[:, 0, 0:48], TP[:, 0, 0:48], ACT.Exp)
            run(TP[:, 0, 128:130], TP[:, 0, 128:130], ACT.Exp, "par_act")
            for n in range(8):
                act.wait_ge(S("x_T"), n + 1)
                run(X[:, 2 * n:2 * n + 2, :], PS[:, n % 4, :].rearrange("p (a t) -> p a t", a=2), sem="x_evac")
            act.wait_ge(S("cact_ready"), 1)
            for k in range(4):
                gemv_window(act, k, k)
            act.wait_ge(S("s5_dt"), 1)
            run(TM[:, 2], TM[:, 2], ACT.Exp, "s5_act")
            act.wait_ge(S("s5_dt"), 2)
            run(TM[:, 3], TM[:, 3], ACT.Exp)
            run(TM[:, 6:8], TM[:, 6:8], ACT.Sin, "s5_act")
            for n in range(8):
                act.wait_ge(S("c_T"), n + 1)
                ci, T2 = n // 2, n % 2
                d, c = ci // 2, ci % 2
                dst = HF[:, 2048 * c:2048 * c + 2048].rearrange("p (k d x) -> p d k x", d=2, x=64)
                run(dst[:, d, 8 * T2:8 * T2 + 8, :], PS[:, n % 4, :].rearrange("p (k x) -> p k x", x=64), sem="c_evac")
            with act.Fori(0, 4) as q:
                for j in range(4):
                    par = j % 2
                    act.wait_ge(S("vpad_ready"), q * 4 + (j + 1))
                    act.wait_ge(S("taps"), q * 4 + (j - 1 + PRIME_TAPS))
                    for c in range(2):
                        for d in range(2):
                            src = Vp[par][:, c, 4 * d:4 * d + 4, 3 * (1 - d), :]
                            ins = run(Rp[par][:, c, 4 * d:4 * d + 4].rearrange("p t (r m) -> p t r m", r=4),
                                      src.unsqueeze(2).broadcast_to([P, 4, 4, 32]))
                    ins.then_inc(S("rp_ready"), 1)
                    act.wait_ge(S("v_T"), q * 4 + (j + 1))
                    act.wait_ge(S("v_stored"), q * 64 + 16 * (j + PRIME_MAT))
                    run(WF[:, 2048:4096], bank(0, 4), sem="vs_ready")
                    act.wait_ge(S("vs_ready"), q * 4 + (j + 1 + PRIME_MAT))
                    act.dma_start(vmat[bass.ds(q * 4 + j, 1)].rearrange("o p m -> p (o m)"),
                                  WF[:, 2048:4096]).then_inc(S("v_stored"), 16)
                    act.wait_ge(S("opad_ready"), q * 4 + (j + 1))
                    for d in range(2):
                        for c in range(2):
                            act.dma_start(
                                omat[bass.ds(q * 5 + (1 + j), 1), :, (2 * d + c) * 512:(2 * d + c + 1) * 512]
                                .rearrange("o p (t m) -> p (o t) m", t=4),
                                Op[par][:, c, 4 * d:4 * d + 4, 1 - d:5 - d, :].rearrange("p t s m -> p t (s m)")
                            ).then_inc(S(f"out_stored{par}"), 16)
                    act.wait_ge(S("taps"), q * 4 + (j + 1 + PRIME_TAPS))
                    if j == 0:
                        act.wait_ge(S("intra_stored"), q * 16 + 16 * PRIME_MAT)
                    for r in range(4):
                        rows_ = slice(32 * r, 32 * r + 32)
                        ins = run(INTRA[rows_, 4 * j:4 * j + 4, 32 * r:P],
                                  PS[rows_, 4, :].rearrange("p (t m) -> p t m", t=4)[:, :, 0:(4 - r) * 32])
                    ins.then_inc(S("intra_f"), 1)
                    if j == 0:
                        act.wait_ge(S("gv0_used"), q * 12 + (16 + PRIME_GV))
                        settle(act)
                        for w in range(3):
                            gemv_window(act, q * 3 + (4 + w), w)
                act.wait_ge(S("intra_ready"), q * 4 + (4 + PRIME_MAT))
                act.dma_start(omat[bass.ds(q * 5, 1)].rearrange("o p m -> p (o m)"),
                              PF[:, 0:2048]).then_inc(S("intra_stored"), 16)

            def h_hi(n, src):
                for g in range(4):
                    act.wait_ge(S("h32"), 4 * n + g + 1)
                    run(Hhi[:, 4 * g:4 * g + 4, :], src[:, 1024 * g:1024 * g + 1024]
                        .rearrange("p (a t) -> p a t", a=4), sem="h_hi")

            def evac(s, blk, par):
                act.wait_ge(S("slab_used"), blk * 4 + (s.G + 4 + PRIME_USED))
                dst = Pb[:, bass.ds(blk * 4 + s.tile0, 4), :]
                src = PS[:, 2 * par:2 * par + 2, :].rearrange("p b (m t) -> p (b m) t", t=T)
                settle(act)
                run(dst, src, s.func, sem="evac_done")
                if s.func == ACT.Relu:
                    act.wait_ge(S("evac_done"), blk + (s.E + 1 + PRIME_EVAC))
                    settle(act)
                    run(dst, dst, ACT.Square, sem="sq_done")

            def split_early(s):
                for sl in range(2):
                    split_hi(act, 0, s.B, s.G, sl)

            def blocks(segs, early=0):
                prev = None
                for s in segs:
                    def body(blk, par, before, skip=0):
                        for sl in range(4):
                            if sl >= skip:
                                split_hi(act, blk, s.B, s.G, sl)
                            if sl == 1 and before is not None:
                                evac(*before, 1 - par)
                    for blk in range(2):
                        body(blk, blk, prev, 0 if blk or s is not segs[0] else early)
                        prev = (s, blk)
                    with act.Fori(1, s.bodies // 2) as i:
                        for par in range(2):
                            body(i * 2 + par, par, (s, i * 2 + (par - 1)))
                    prev = (s, s.bodies - 1)
                evac(*prev, 1)

            def down_hi(s, n):
                with act.Fori(0, 8) as i:
                    for sl in range(4):
                        split_hi(act, i, s.B, s.G, sl)
                        run(Hhi[:, 2 * (sl % 2):2 * (sl % 2) + 2, :], Pb[:, bass.ds(i * 8 + 2 * sl, 2), :],
                            sem="hx_hi")

            def layer_norm_act(k):
                for g in range(4):
                    act.wait_ge(S("ln_cent"), 4 * k + g + 1)
                    run(PF[:, 1024 * g:1024 * (g + 1)], X[:, 4 * g:4 * g + 4].rearrange("p k t -> p (k t)"),
                        ACT.Square, "ln_sq")
                act.wait_ge(S("ln_psum"), 2 * k + 2)
                run(LNS, PS[:, 5, 0:T], ACT.Sqrt, "ln_std", scale=1.0 / D, bias=eps[:, 0:1])

            def rms_act(n, o):
                run(SQ, o, ACT.Square, "rms_sq")
                if n == 1:
                    run(PF[:, 8192:12288], PF[:, 8192:12288], ACT.Sigmoid, "hg_sig")
                act.wait_ge(S("rms_sum"), n)
                run(RS[0:ROWS, 0:T], PS[0:ROWS, 0, 0:T], ACT.Sqrt, "rms_std", scale=1.0 / P, bias=eps[0:ROWS, 1:2])

            products = [0]

            def ada_products(count):
                first = products[0]
                products[0] += count
                for c in range(first, first + count):
                    act.wait_ge(S(f"pool_ready{c % 3}"), 16 * (c // 3 + 1))
                    run(araw[:, c % 3, :], araw[:, c % 3, :], scale=cact[:, c // 6:c // 6 + 1], sem="ada_product")

            def attention_act():
                run(CW[:, 3, ROWS - 1:ROWS], ones[:, 0:1], sem="cw_ready")
                for g in range(8):
                    act.wait_ge(S("vt_T"), g + 1)
                    dst = (HF[:, 0:2048] if g < 4 else PF[:, 4096:6144])[:, 512 * (g % 4):512 * (g % 4) + 512]
                    run(dst, PS[:, g % 4, :], sem="vt_evac")

                def exps(n):
                    par = n % 2
                    act.wait_ge(S("at_max"), n + 1)
                    if n >= 2:
                        act.wait_ge(S("at_T"), n - 1)
                    for c in range(2):
                        ins = run(EA[:, par, c, :], PS[:, 2 * par + c, 0:T], ACT.Exp, scale=QK_SCALE,
                                  bias=nm[par][:, c:c + 1], accum_out=sm[par][:, c:c + 1])
                    ins.then_inc(S("at_exp"), 1)

                ada_products(6)
                exps(0)
                exps(1)
                for n in range(16):
                    h, qt, par = n // 2, n % 2, n % 2
                    act.wait_ge(S("at_T"), n + 1)
                    run(AT[:, par], PS[:, 4 + par, 0:T].rearrange("p (a t) -> p a t", a=2), sem="at_Te")
                    ada_products(1)
                    if n < 14:
                        exps(n + 2)
                    act.wait_ge(S("at_pv"), n + 1)
                    link(run(Pb[:, h, qt * P:(qt + 1) * P], PS[:, 6 + par, 0:P]))
                    ada_products(1)
                rms_act(1, OA)

            def hgrn_act():
                act.wait_ge(S("oa_final"), 1)
                run(EX[0], QH, ACT.Sigmoid)
                run(EX[1], GH, ACT.Sigmoid, "hg_sig")
                ada_products(4)
                for d in range(2):
                    act.wait_ge(S("hg_f"), d + 1)
                    run(EX[d], EX[d], ACT.Ln, "hg_ln")
                    ada_products(3)
                for n in range(16):
                    act.wait_ge(S("lv_arg"), n + 1)
                    run(EX[n % 3], EX[n % 3], ACT.Exp, "lv_exp")
                    ada_products(3)
                act.wait_ge(S("hg_pv"), 1)
                link(run(OB, bank(4, 4)))
                rms_act(2, OB)
                act.wait_ge(S("o_ready"), 1)
                run(Hhi[:, 0:8, :], Pb[:, 0:8, :], sem="o_hi")
                run(Hhi[:, 8:16, :], Pb[:, 32:40, :], sem="o_hi")

            def s5_act():
                for n in range(16):
                    act.wait_ge(S("mat_used"), n + 1)
                    for c in range(2):
                        ins = run(SV[:, :, c, 8 * n:8 * n + 8].rearrange("p n x -> p x n"),
                                  PS[:, 2 * (n % 4) + c, :].rearrange("p (x n) -> p x n", x=8))
                    ins.then_inc(S("sv_evac"), 1)
                act.wait_ge(S("pool_summed"), 1)
                for w in range(2):
                    gemv_window(act, w, w)
                with act.Fori(1, KT // 2) as kk:
                    for w in range(2):
                        act.wait_ge(S("gv2_used"), kk * 8 + (4 * w - 4 + PRIME_GV))
                        settle(act)
                        gemv_window(act, kk * 2 + w, w)
                for q in range(4):
                    gs = slice(1024 * q, 1024 * (q + 1))
                    act.wait_ge(S("ge_in"), 2 * q + 1)
                    run(WF[:, gs], HF[:, gs], ACT.Square, "ge_sq")
                    act.wait_ge(S("ge_in"), 2 * q + 2)
                    run(WF[:, gs], WF[:, gs], ACT.Sigmoid, "ge_sig", scale=2 * GELU_C)
                for g in range(4):
                    act.wait_ge(S(f"g_ready{g}"), 256)
                    run(Hhi[:, 4 * g:4 * g + 4, :].rearrange("p k t -> p (k t)"), GLF[:, 1024 * g:1024 * (g + 1)],
                        sem="o_hi")

            h_hi(0, PF[:, 4096:8192])
            for s in plan_in:
                s.func, s.tile0 = ACT.Copy, 4 * (s.E - plan_in[0].E)
            blocks(plan_in)
            act.wait_ge(S("evac_done"), PRIME_EVAC + 16)
            act.sem_inc(S("in_done"), 1)
            attention_act()
            hgrn_act()
            act.wait_ge(S("pool_summed"), 1)
            for s in plan_out:
                with act.Fori(0, s.bodies) as i:
                    for sl in range(4):
                        split_hi(act, i, s.B, s.G, sl)
            split_early(plan_mlp[0][0][0])
            layer_norm_act(0)
            h_hi(1, PF[:, 4096:8192])
            for layer in range(2):
                if layer == 1:
                    s5_act()
                    for n, s in enumerate(plan_glu):
                        s.func, s.tile0 = (ACT.Copy, ACT.Sigmoid)[n], 16 + 16 * n
                    blocks(plan_glu)
                    split_early(plan_mlp[1][0][0])
                    layer_norm_act(2)
                    h_hi(2, PF[:, 4096:8192])
                up, dn = plan_mlp[layer]
                for n, s in enumerate(up):
                    s.func, s.tile0 = ACT.Relu, 32 * n
                blocks(up, early=2)
                act.wait_ge(S("sq_done"), 16 * (layer + 1))
                for s in dn:
                    down_hi(s, 2 * layer + s.half)
                layer_norm_act(1 + 2 * layer)
            for n in range(8):
                act.wait_ge(S("o_T"), n + 1)
                ins = run(ON[:, n // 4, (n % 4) * 512:(n % 4 + 1) * 512], PS[:, n, :])
                if n % 4 == 3:
                    ins.then_inc(S("out_ready"), 1)

        @block.vector
        def _(v):
            link = chain(v, "dve_chain")
            tt, ts, stt = nc.vector.tensor_tensor, nc.vector.tensor_scalar, nc.vector.scalar_tensor_tensor
            v.sem_inc(S("lo_done"), PRIME_RAW)
            v.sem_inc(S("intra_ready"), PRIME_MAT)
            for u, (_, _, halves) in enumerate(ADA):
                v.sem_inc(S(f"ada{u}_used"), halves)
            link(nc.vector.memset(WF[:, 0:512], 0.0))
            v.sem_inc(S("stg_zero"), 1)
            for ap, x in ((ones[:], 1.0), (small[:], 0.0), (CW[:], 0.0), (eps[:, 0:1], LN_EPS), (eps[:, 1:2], RMS_EPS)):
                link(nc.vector.memset(ap, x))
            v.sem_inc(S("ones_ready"), 1)
            for par in range(2):
                link(nc.vector.memset(V_AREAS[par], 0.0))
            v.wait_ge(S("par_T"), 1)
            link(nc.vector.tensor_copy(PT[:].rearrange("p a c -> p (a c)"), PS[:, 6, :]))
            lb3 = LBR.rearrange("p (d l m) -> p l d m", d=2, l=3)
            e3 = TP[:, 0, 0:48].rearrange("p (l d m) -> p l d m", l=3, d=2)
            m3 = TP[:, 0, 64:80].rearrange("p (d m) -> p d m", d=2)
            link(tt(m3, lb3[:, 0], lb3[:, 1], ALU.max))
            link(tt(m3, m3, lb3[:, 2], ALU.max))
            for l in range(3):
                link(tt(e3[:, l], lb3[:, l], m3, ALU.subtract))
            v.wait_ge(S("ld_par"), 9 * 16)
            for k in range(2):
                link(tt(LT[:, k], LAMR[:, 2 * k], LAMR[:, 2 * k + 1], ALU.mult))
            link(nc.vector.tensor_reduce(TP[:, 0, 128:130], LT, AX.X, ALU.add))
            v.sem_inc(S("par_ready"), 1)
            v.wait_ge(S("par_act"), 1)
            link(tt(cact[:], cact[:], CRAW, ALU.mult))
            v.sem_inc(S("cact_ready"), 1)
            link(tt(m3, e3[:, 0], e3[:, 1], ALU.add))
            link(tt(m3, m3, e3[:, 2], ALU.add))
            link(nc.vector.reciprocal(TP[:, 0, 64:80], TP[:, 0, 64:80]))
            link(tt(lbs[:, :, 0:8], e3[:, 0], m3, ALU.mult))
            link(ts(lbs[:, :, 8:16], lbs[:, :, 0:8], -1.0, 1.0, ALU.mult, ALU.add))
            link(tt(lamb[:, 1:2], TP[:, 0, 129:130], TP[:, 0, 128:129], ALU.subtract))
            link(ts(lamb[:, 0:1], lamb[:, 1:2], -LAM_INIT, None, ALU.add))
            link(ts(SUBG, SUBG, 1.0 - LAM_INIT, None, ALU.mult))
            v.wait_ge(S("ld_s5"), 10 * 16)
            for d in range(2):
                link(nc.vector.tensor_copy(LS[0:64, 4 + d, :].rearrange("p (g x) -> p g x", g=2),
                                           LDT[0:64, d, :].unsqueeze(2).broadcast_to([64, 2, 64])))
            v.sem_inc(S("ls_ready"), 1)
            v.wait_ge(S("ls_T"), 1)
            for k in range(3):
                for d in range(2):
                    link(nc.vector.tensor_copy(
                        TM[:, k].rearrange("p (c d t) -> p d c t", d=2, t=4)[:, d],
                        PS[:, 5, (2 * k + d) * 64:(2 * k + d + 1) * 64].rearrange("p (c t) -> p c t", t=4)))
            link(nc.vector.tensor_copy(Dsk[:], PS[:, 5, 384:448]))
            v.sem_inc(S("ls_evac"), 1)
            v.sem_inc(S("s5_dt"), 1)
            LR, LI, DT, T3, T4, T5, T6, T7 = (TM[:, k] for k in range(8))
            v.wait_ge(S("s5_act"), 1)
            link(tt(T3, LR, DT, ALU.mult))
            link(tt(T4, LI, DT, ALU.mult))
            two_pi = 2 * math.pi
            c1 = float(np.float32(6.28125))
            c2 = float(np.float32(np.float32((two_pi - c1) * 2 ** 20).astype(np.int64) / 2 ** 20))
            c3 = two_pi - c1 - c2
            for dst, shift in ((T6, 0.0), (T7, 0.25)):
                link(ts(T5, T4, 1 / two_pi, shift, ALU.mult, ALU.add))
                link(ts(T5, T5, MAGIC, None, ALU.add))
                link(ts(T5, T5, -MAGIC, None, ALU.add))
                link(stt(dst, T5, -c1, T4, ALU.mult, ALU.add))
                link(stt(dst, T5, -c2, dst, ALU.mult, ALU.add))
                link(stt(dst, T5, -c3, dst, ALU.mult, ALU.add))
                if shift:
                    link(ts(dst, dst, math.pi / 2, None, ALU.add))
                pi_ = float(np.nextafter(np.float32(math.pi), np.float32(0)))
                link(ts(dst, dst, pi_, -pi_, ALU.min, ALU.max))
            v.sem_inc(S("s5_dt"), 1)
            v.wait_ge(S("s5_act"), 2)
            AR, AI = PW[:, 0, 0], PW[:, 0, 1]
            link(tt(AR, T3, T7, ALU.mult))
            link(tt(AI, T3, T6, ALU.mult))
            link(tt(T3, LR, LR, ALU.mult))
            link(tt(T4, LI, LI, ALU.mult))
            link(tt(T3, T3, T4, ALU.add))
            link(nc.vector.reciprocal(T3, T3))
            link(ts(T5, AR, -1.0, None, ALU.add))
            link(tt(T6, T5, LR, ALU.mult))
            link(tt(T7, AI, LI, ALU.mult))
            link(tt(T6, T6, T7, ALU.add))
            link(tt(T6, T6, T3, ALU.mult))
            link(tt(T7, AI, LR, ALU.mult))
            link(tt(T4, T5, LI, ALU.mult))
            link(tt(T7, T7, T4, ALU.subtract))
            link(tt(T7, T7, T3, ALU.mult))
            v.wait_ge(S("ld_b"), 256)
            bc = [t_.unsqueeze(2).broadcast_to([P, P, 16]) for t_ in (T6, T7)]
            tmp = PF[:, 0:2048].rearrange("p (x h) -> p x h", h=16)
            for c in range(2):
                link(tt(tmp, bc[1], Bn[:, 1 - c], ALU.mult))
                link(tt(BB[:, c], bc[0], Bn[:, c], ALU.mult))
                link(tt(BB[:, c], BB[:, c], tmp, ALU.subtract if c == 0 else ALU.add))
            for k in range(1, 4):
                pr, pi = PW[:, k - 1, 0], PW[:, k - 1, 1]
                link(tt(T3, pr, AR, ALU.mult))
                link(tt(T4, pi, AI, ALU.mult))
                link(tt(PW[:, k, 0], T3, T4, ALU.subtract))
                link(tt(T3, pr, AI, ALU.mult))
                link(tt(T4, pi, AR, ALU.mult))
                link(tt(PW[:, k, 1], T3, T4, ALU.add))
            for k, (c, f) in enumerate(((0, 1.0), (0, 1.0), (1, 1.0), (1, -1.0))):
                link(ts(A4[:, k, :], PW[:, 3, c], f, None, ALU.mult))
            v.wait_ge(S("c_evac"), 8)
            link(nc.vector.memset(PF[:, 10240:13184], 0.0))
            for e in range(5):
                for d in range(2):
                    for c in range(3):
                        def slot(arr, c_, k):
                            return arr[:, c_, :, k].rearrange("p (c d t) -> p d c t", d=2, t=4)[:, d]
                        spots = [slot(PWO, c, e if d == 0 else 4 - e)]
                        if c < 2 and e < 4:
                            spots.append(slot(PWV, c, 3 - e if d == 0 else e))
                        for sp_ in spots:
                            if e == 0:
                                if c != 1:
                                    link(nc.vector.memset(sp_, 1.0 if c == 0 else -1.0))
                            else:
                                link(ts(sp_, PW[:, e - 1, c % 2].rearrange("p (c d t) -> p d c t", d=2, t=4)[:, d],
                                        -1.0 if c == 2 else 1.0, None, ALU.mult))
            v.sem_inc(S("pw_ready"), 1)

            def intra_sums(lk, q, j):
                v.wait_ge(S("taps"), q * 4 + (j + 1 + PRIME_TAPS))
                v.wait_ge(S("intra_f"), q * 4 + (j + 1))
                ps = PS[:, 5, :].rearrange("p (t m) -> p t m", t=4)
                tl = slice(4 * j, 4 * j + 4)
                for r in range(4):
                    R_ = slice(32 * r, 32 * r + 32)
                    if r:
                        lk(nc.vector.tensor_copy(INTRA[R_, tl, 0:32 * r], ps[R_, :, (3 - r) * 32:96]))
                    lk(tt(INTRA[R_, tl, 32 * r:32 * r + 32], INTRA[R_, tl, 32 * r:32 * r + 32],
                          ps[R_, :, 96:128], ALU.add))
                v.sem_inc(S("intra_ready"), 1)

            with v.Fori(0, 4) as q:
                lk = stepper(v, "v_steps", q, 4 * (8 + 7))
                for j in range(4):
                    pad(nc.vector, lk, Vp[j % 2], TP, PWV, BB, q * 32 + 8 * j, 4, (0, 1, 0))
                    v.sem_inc(S("vpad_ready"), 1)
                    if j:
                        intra_sums(lk, q, j - 1)
                intra_sums(lk, q, 3)
            gemv_copy(v, link, 0, "gv0_used", 64 + PRIME_GV)
            gemv_finish(v, link, 0)
            link(nc.vector.memset(acc[:], 0.0))

            def modulation(sub, k):
                if sub in (1, 2):
                    link(ts(G1[:, sub], MOD[:, sub, 32:48], 1.0, None, ALU.add))
                link(ts(HA[:, 0], MOD[:, sub, 16:32], 1.0, None, ALU.add))
                if k is None:
                    link(nc.vector.tensor_copy(HA[:, 1], MOD[:, sub, 0:16]))
                    link(nc.vector.memset(XAB[:, 0], ALPHA))
                    link(nc.vector.memset(XAB[:, 1], 0.0))
                else:
                    link(tt(HA[:, 1], HA[:, 0], LNB[k], ALU.mult))
                    link(tt(HA[:, 1], HA[:, 1], MOD[:, sub, 0:16], ALU.add))
                    link(tt(HA[:, 0], HA[:, 0], LNG[k], ALU.mult))
                    link(ts(XAB[:, 0], LNG[k], ALPHA, None, ALU.mult))
                    link(ts(XAB[:, 1], LNB[k], ALPHA, None, ALU.mult))
                v.sem_inc(S("xab_ready"), 1)

            h32 = PF[:, 4096:8192].rearrange("p (k t) -> p k t", t=T)

            def make_h(n, norm=None):
                def low(g):
                    v.wait_ge(S("h_hi"), 4 * n + g + 1)
                    gs = slice(4 * g, 4 * g + 4)
                    tt(Hlo[:, gs], h32[:, gs], Hhi[:, gs].bitcast(F), ALU.subtract).then_inc(S("h_ready"), 1)
                for g in range(4):
                    if norm is not None:
                        normalise(slice(4 * g, 4 * g + 4))
                    for k in range(4):
                        kt = 4 * g + k
                        ins = ts(h32[:, kt], X[:, kt], HA[:, 0, kt:kt + 1], HA[:, 1, kt:kt + 1], ALU.mult, ALU.add)
                    ins.then_inc(S("h32"), 1)
                    if g:
                        low(g - 1)
                low(3)

            def normalise(ks):
                n = ks.stop - ks.start
                link(tt(X[:, ks], X[:, ks], LNS.unsqueeze(1).broadcast_to([P, n, T]), ALU.mult))

            def layer_norm(k, after=None):
                link(nc.vector.tensor_reduce(LNS, X[:].rearrange("p k t -> p t k"), AX.X, ALU.add))
                v.sem_inc(S("ln_sum"), 1)
                v.wait_ge(S("ln_psum"), 2 * k + 1)
                for g in range(4):
                    gs = slice(4 * g, 4 * g + 4)
                    stt(X[:, gs], PS[:, 4, 0:T].unsqueeze(1).broadcast_to([P, 4, T]), -1.0 / D, X[:, gs],
                        ALU.mult, ALU.add).then_inc(S("ln_cent"), 1)
                v.wait_ge(S("ln_cent"), 4 * k + 4)
                if after:
                    for sl in range(2):
                        split_lo(v, 0, after.B, after.G, sl)
                v.wait_ge(S("ln_std"), k + 1)
                link(nc.vector.reciprocal(LNS, LNS))

            def split_lows(segs, fin=None, down=None, early=0):
                for s in segs:
                    def body(i, first):
                        nonlocal fin
                        order = {0: [], 1: [], 2: [0, 1], 3: [2]} if first else {0: [0], 1: [], 2: [1], 3: [2]}
                        if s.ada and ADA[s.ada[0]][2] == 2:
                            order = {0: [], 1: [0], 2: [], 3: [1]}
                        for sl in range(4):
                            if not (first and s is segs[0] and sl < early):
                                split_lo(v, i, s.B, s.G, sl)
                            if down is not None:
                                v.wait_ge(S("hx_hi"), i * 4 + ((down + s.half) * 32 + sl + 1))
                                hs = slice(2 * (sl % 2), 2 * (sl % 2) + 2)
                                tt(Hlo[:, hs], Pb[:, bass.ds(i * 8 + 2 * sl, 2), :], Hhi[:, hs].bitcast(F),
                                   ALU.subtract).then_inc(S("hx_lo"), 1)
                            if first and sl == 1:
                                if down is not None and s.half:
                                    evac_down(segs[0], down)
                                if fin:
                                    ada_finish(v, link, fin.ada[0], 4)
                                    fin = None
                            if s.ada:
                                for r in order[sl]:
                                    ada_mac(v, i, *s.ada, r)
                    body(0, True)
                    with v.Fori(1, s.bodies) as i:
                        body(i, False)
                    if s.ada and s.ada[1]:
                        fin = s
                return fin

            def evac_down(s, n):
                v.wait_ge(S("x_scaled"), n + 2)
                v.wait_ge(S("slab_used"), s.G + 32 + PRIME_USED)
                for m in range(8):
                    kt = 8 * s.half + m
                    ins = stt(X[:, kt], PS[:, 4 * s.half + m // 2, (m % 2) * T:(m % 2 + 1) * T],
                              G1[:, n + 1, kt:kt + 1], X[:, kt], ALU.mult, ALU.add)
                ins.then_inc(S("down_evac"), 1)
                v.wait_ge(S("down_evac"), n + s.half + 1)

            modulation(0, None)
            v.wait_ge(S("x_evac"), 8)
            v.wait_ge(S("v_stored"), 256 + 16 * PRIME_MAT)
            for par in range(2):
                v.wait_ge(S(f"out_stored{par}"), 64 * (8 + PRIME_MAT))
            v.wait_ge(S("intra_stored"), 64 + 16 * PRIME_MAT)
            make_h(0)
            fin = split_lows(plan_in)
            ada_finish(v, link, fin.ada[0], 4)

            v.wait_ge(S("ld_rot"), 64)
            v.wait_ge(S("in_done"), 1)
            cs, sn = (z.unsqueeze(1).broadcast_to([P, 2, T]) for z in (COS, SIN))
            for n in range(8):
                v.wait_ge(S("rot_mm"), n + 1)
                qk = Pb[:, 2 * n:2 * n + 2, :]
                link(tt(ROTT, PS[:, 4 + n % 2, :].rearrange("p (b t) -> p b t", b=2), sn, ALU.mult))
                link(tt(qk, qk, cs, ALU.mult))
                link(tt(qk, qk, ROTT, ALU.add))
                v.sem_inc(S("rot_done"), 1)

            def rms_scale(n, o, g):
                v.wait_ge(S("rms_std"), n)
                link(nc.vector.reciprocal(RS[0:ROWS, 0:T], RS[0:ROWS, 0:T]))
                v.sem_inc(S("rms_inv"), 1)
                v.wait_ge(S("rms_wide"), n)
                link(stt(o, o, g, bank(0, 4), ALU.mult, ALU.mult))

            def row_max(n):
                par = n % 2
                v.wait_ge(S("at_score"), n + 1)
                link(nc.vector.tensor_reduce(mx[par], PS[:, 2 * par:2 * par + 2, 0:T], AX.X, ALU.max))
                link(ts(nm[par], mx[par], -QK_SCALE, None, ALU.mult))
                v.sem_inc(S("at_max"), 1)

            def mix(n):
                par = n % 2
                v.wait_ge(S("at_exp"), n + 1)
                link(nc.vector.reciprocal(rc[par], sm[par]))
                link(tt(rc[par][:, 1:2], rc[par][:, 1:2], lamb[:, 0:1], ALU.mult))
                link(ts(EA[:, par, 1], EA[:, par, 1], rc[par][:, 1:2], None, ALU.mult))
                link(stt(EA[:, par, 0], EA[:, par, 0], rc[par][:, 0:1], EA[:, par, 1], ALU.mult, ALU.add))
                v.sem_inc(S("at_mix"), 1)

            row_max(0)
            row_max(1)
            for n in range(16):
                mix(n)
                if n < 14:
                    row_max(n + 2)
            link(nc.vector.memset(SCDF, 0.0))
            rms_scale(1, OA, SUBG)
            v.sem_inc(S("oa_final"), 1)

            v.wait_ge(S("hg_sig"), 2)
            link(tt(QH, QH, EX[0], ALU.mult))
            link(tt(GH, GH, EX[1], ALU.mult))
            for d, ff in enumerate((FF_, FB_)):
                for h in range(8):
                    hs = slice(h * T, (h + 1) * T)
                    link(ts(EX[d][:, hs], ff[:, hs], lbs[:, d, 8 + h:9 + h], lbs[:, d, h:h + 1], ALU.mult, ALU.add))
                link(ts(ff, EX[d], -1.0, 1.0, ALU.mult, ALU.add))
                v.sem_inc(S("hg_f"), 1)
            for d in range(2):
                v.wait_ge(S("hg_ln"), d + 1)
                if d:
                    link(nc.vector.memset(LC[1].rearrange("p (h t) -> p h t", h=8)[:, :, 0:1], 0.0))
                for h in range(8):
                    link(nc.vector.tensor_tensor_scan(LC[d][:, h * T + d:(h + 1) * T], ones[:, 0:T - d],
                                                      EX[d][:, h * T:(h + 1) * T - d], 0.0, ALU.mult, ALU.add))

            def level_views(ap, half):
                z = ap.rearrange("p (b u q) -> p u b q", u=2, q=half)
                return z[:, 0], z[:, 1]

            def level_arg(n):
                lv, d = n // 2, n % 2
                half = 2 ** lv
                if n >= 3:
                    v.wait_ge(S("lv_mm"), n - 2)
                left, right = level_views(LC[d], half)
                oleft, oright = level_views(EX[n % 3], half)
                at = left[:, :, half - 1:half] if d == 0 else right[:, :, 0:1]
                at = at.broadcast_to([P, 1024 // half, half])
                link(tt(oleft, at, left, ALU.subtract))
                link(tt(oright, right, at, ALU.subtract))
                v.sem_inc(S("lv_arg"), 1)

            def level_mul(n):
                lv, d = n // 2, n % 2
                half = 2 ** lv
                if n < 16:
                    v.wait_ge(S("lv_exp"), n + 1)
                    oleft, oright = level_views(EX[n % 3], half)
                    kl, kr = level_views((FF_, FB_)[d], half)
                    ql, qr = level_views(QH, half)
                    link(tt(oleft, oleft, kl if d == 0 else ql, ALU.mult))
                    link(tt(oright, oright, qr if d == 0 else kr, ALU.mult))
                else:
                    v.wait_ge(S("lv_mm"), n - 2)
                    link(tt(EX[n % 3], FF_, FB_, ALU.add))
                v.sem_inc(S("lv_x"), 1)

            def level_put(n):
                lv, d = n // 2, n % 2
                v.wait_ge(S("lv_mm"), n + 1)
                b0 = 4 * (n % 2)
                if lv == 7:
                    link(nc.vector.tensor_copy(SCO[:, d].rearrange("p h t -> p (h t)"), bank(b0, 2)))
                else:
                    m = 14 if n == 16 else 7 * d + lv
                    link(nc.vector.copy_predicated(SCD, MASKS[:, m, :].unsqueeze(1).broadcast_to([P, 16, P]),
                                                   bank(b0, 4).rearrange("p (x t) -> p x t", x=16)))
                v.sem_inc(S("lv_put"), 1)

            level_arg(0)
            for n in range(17):
                if n < 15:
                    level_arg(n + 1)
                level_mul(n)
                if n:
                    level_put(n - 1)
            level_put(16)
            rms_scale(2, OB, HGG)
            link(tt(OB, OB, GH, ALU.mult))
            v.sem_inc(S("o_ready"), 1)
            for k, o in enumerate((Pb[:, 0:8, :], Pb[:, 32:40, :])):
                v.wait_ge(S("o_hi"), k + 1)
                tt(Hlo[:, 8 * k:8 * k + 8], o, Hhi[:, 8 * k:8 * k + 8].bitcast(F), ALU.subtract
                   ).then_inc(S("h_ready"), 2)

            gemv_copy(v, link, 1, "pool_summed", 1)
            gemv_finish(v, link, 1)
            link(nc.vector.memset(acc[:], 0.0))

            s = plan_out[0]

            def evac_out(blk):
                v.wait_ge(S("slab_used"), s.G + 4 * blk + 4 + PRIME_USED)
                for m in range(4):
                    kt = 4 * blk + m
                    ins = stt(X[:, kt], PS[:, 2 * (blk % 2) + m // 2, (m % 2) * T:(m % 2 + 1) * T],
                              G1[:, 0, kt:kt + 1], X[:, kt], ALU.mult, ALU.add)
                ins.then_inc(S("evac_done"), 1)
            v.wait_ge(S("x_scaled"), 1)
            for blk in range(4):
                for sl in range(4):
                    split_lo(v, blk, s.B, s.G, sl)
                    if sl == 1 and blk:
                        evac_out(blk - 1)
            evac_out(3)
            v.wait_ge(S("evac_done"), s.E + 4 + PRIME_EVAC)
            modulation(1, 0)
            layer_norm(0, plan_mlp[0][0][0])
            make_h(1, 0)
            for layer in range(2):
                if layer == 1:
                    for half in range(2):
                        v.wait_ge(S(f"u_ready{half}"), 256)
                    link(tt(YT, UT, Dsk[:].unsqueeze(2).broadcast_to([P, 64, 64]), ALU.mult))
                    v.wait_ge(S("sv_evac"), 16)
                    A4v = A4[:].rearrange("p (a c) x -> p a c x", a=2)
                    with v.Fori(1, 63) as k:
                        old, new = SV[:, bass.ds(k - 1, 1)], SV[:, bass.ds(k, 1)]
                        old, new = (z.rearrange("p n c x -> p (n c) x") for z in (old, new))
                        tt(STP[:, 0], A4v[:, 0], old, ALU.mult).then_inc(S("scan_steps"), 1)
                        tt(STP[:, 1], A4v[:, 1], old, ALU.mult).then_inc(S("scan_steps"), 1)
                        v.wait_ge(S("scan_steps"), k * 4 - 3)
                        tt(new, new, STP[:, 0], ALU.add).then_inc(S("scan_steps"), 1)
                        v.wait_ge(S("scan_steps"), k * 4 - 1)
                        tt(new, new, STP[:, 1, ::-1], ALU.add).then_inc(S("scan_steps"), 1)
                        v.wait_ge(S("scan_steps"), k * 4)
                    v.sem_inc(S("s5_scan"), 1)
                    gemv_copy(v, link, 2, "gv2_used", 64 + PRIME_GV)
                    gemv_finish(v, link, 2)
                    link(nc.vector.memset(acc[:], 0.0))
                    for q in range(4):
                        v.wait_ge(S("mat_used"), 16 + 5 * (q + 1))
                        gs = slice(1024 * q, 1024 * (q + 1))
                        yq, t_ = HF[:, gs], WF[:, gs]
                        link(tt(yq, yq, bank(2 * q, 2), ALU.add))
                        v.sem_inc(S("ge_in"), 1)
                        v.wait_ge(S("ge_sq"), q + 1)
                        link(ts(t_, t_, 0.044715, 1.0, ALU.mult, ALU.add))
                        link(tt(t_, t_, yq, ALU.mult))
                        v.sem_inc(S("ge_in"), 1)
                        v.wait_ge(S("ge_sig"), q + 1)
                        link(tt(yq, yq, t_, ALU.mult))
                        v.sem_inc(S("y_ready"), 1)
                    for g in range(4):
                        v.wait_ge(S("o_hi"), 3 + g)
                        gs = slice(4 * g, 4 * g + 4)
                        tt(Hlo[:, gs].rearrange("p k t -> p (k t)"), GLF[:, 1024 * g:1024 * (g + 1)],
                           Hhi[:, gs].rearrange("p k t -> p (k t)").bitcast(F), ALU.subtract
                           ).then_inc(S("h_ready"), 1)
                    v.wait_ge(S("h_ready"), 16)
                    split_lows(plan_glu)
                    v.wait_ge(S("evac_done"), plan_glu[1].E + 4 + PRIME_EVAC)
                    v.wait_ge(S("x_scaled"), 3)
                    link(tt(PF[:, 4096:8192], PF[:, 4096:8192], PF[:, 8192:12288], ALU.mult))
                    for kt in range(KT):
                        xv = X[:, kt].rearrange("p (n j) -> p j n", j=4)
                        link(stt(xv, Pb[:, 16 + kt].rearrange("p (j n) -> p j n", j=4), G1[:, 2, kt:kt + 1], xv,
                                 ALU.mult, ALU.add))
                    modulation(3, 2)
                    layer_norm(2, plan_mlp[1][0][0])
                    make_h(2, 2)
                up, dn = plan_mlp[layer]
                fin = split_lows(up, early=2)
                fin = split_lows(dn, fin=fin, down=2 * layer)
                evac_down(dn[1], 2 * layer)
                if fin:
                    ada_finish(v, link, fin.ada[0], 0)
                if layer == 0:
                    modulation(2, 1)
                layer_norm(1 + 2 * layer)
                if layer:
                    normalise(slice(0, KT))
                else:
                    for half in range(2):
                        normalise(slice(8 * half, 8 * half + 8))
                        for kt in range(8 * half, 8 * half + 8):
                            ins = ts(HS[:, kt].rearrange("p j n -> p n j"),
                                     X[:, kt].rearrange("p (n j) -> p n j", j=4),
                                     HA[:, 0, kt:kt + 1], HA[:, 1, kt:kt + 1], ALU.mult, ALU.add)
                        ins.then_inc(S("hs_ready"), 1)
            for kt in range(KT):
                ins = ts(X[:, kt], X[:, kt], LNG[3][:, kt:kt + 1], LNB[3][:, kt:kt + 1], ALU.mult, ALU.add)
            link(ins)
            v.sem_inc(S("x_final"), 1)

        @block.gpsimd
        def _(pool):
            for par in range(2):
                nc.gpsimd.memset(O_AREAS[par], 0.0).then_inc(S("opad_zero"), 1)
            pool.wait_ge(S("opad_zero"), 2)
            pool.wait_ge(S("pw_ready"), 1)
            with pool.Fori(0, 8) as m:
                lk = stepper(pool, "p_steps", m, 16)
                for par in range(2):
                    pool.wait_ge(S("taps"), m * 2 + (par - 1 + PRIME_TAPS))
                    pool.wait_ge(S(f"out_stored{par}"), m * 64 + 64 * PRIME_MAT)
                    pad(nc.gpsimd, lk, Op[par], TG, PWO, CTt, m * 16 + 8 * par, 5, (0, 1, 2))
                    pool.sem_inc(S("opad_ready"), 1)
            pool.sem_inc(S("pool_used"), 3)
            pool.wait_ge(S("in_done"), 1)
            nc.gpsimd.memset(PACC, 0.0).then_inc(S("pool_zero"), 1)
            pool.wait_ge(S("pool_zero"), 1)
            with pool.Fori(0, KT) as k:
                for r in range(6):
                    pool.wait_ge(S("ada_product"), k * 6 + (r + 1))
                    pool.wait_ge(S("pool_used"), k * 6 + (r + 3))
                    settle(pool)
                    cols = PACC[:, r * ADA_HALF:(r + 1) * ADA_HALF]
                    nc.gpsimd.tensor_tensor(cols, cols, araw[:, r % 3, :], ALU.add).then_inc(S("pool_used"), 1)
            for k in range(4):
                pool.wait_ge(S("xab_ready"), k + 1)
                if k == 2:
                    pool.wait_ge(S("hs_ready"), 2)
                else:
                    pool.wait_ge(S("h32"), 4 * (k if k < 3 else 2) + 4)
                for kt in range(KT):
                    ins = nc.gpsimd.tensor_scalar(X[:, kt], X[:, kt], XAB[:, 0, kt:kt + 1], XAB[:, 1, kt:kt + 1],
                                                  ALU.mult, ALU.add)
                ins.then_inc(S("x_scaled"), 1)


NAMES = ["x", "c", "ada_w", "ada_b", "ln_g", "ln_b", "mix_w_in", "mix_w_out", "diff_lambda", "diff_subln_g",
         "hg_lower_bound", "hg_norm_g", "s5_lambda_re", "s5_lambda_im", "s5_log_dt", "s5_b_re", "s5_b_im",
         "s5_c_re", "s5_c_im", "s5_d", "s5_w_glu", "mlp_w1", "mlp_w2"]


def constants():
    ident = np.eye(P, dtype=np.float32)
    rot = np.zeros((P, P), np.float32)
    cos, sin = np.ones((P, T), np.float32), np.zeros((P, T), np.float32)
    inv = (1.0 / (np.float32(500000.0) ** (np.arange(0, 16, 2, dtype=np.float32) / np.float32(16)))).astype(np.float32)
    ang = (np.arange(T, dtype=np.float32)[:, None] * inv[None, :]).astype(np.float32).T
    for c in range(2):
        for r in range(8):
            lo, hi = 64 * c + r, 64 * c + 8 + r
            rot[hi, lo], rot[lo, hi] = -1.0, 1.0
            cos[lo] = cos[hi] = np.cos(ang[r])
            sin[lo] = sin[hi] = np.sin(ang[r])
    s, t = np.meshgrid(np.arange(P), np.arange(P), indexing="ij")
    masks = np.zeros((15, P, P), np.float32)
    for lv in range(7):
        apart = ((s >> lv) ^ (t >> lv)) == 1
        masks[lv], masks[7 + lv] = apart & (s < t), apart & (s > t)
    masks[14] = s == t
    return {"ident": ident, "rot": rot, "cos": cos, "sin": sin, "masks": masks}


def kernel(**inputs):
    import concourse.bacc as _bacc
    from concourse.bass_utils import run_bass_kernel_spmd as _run

    nc = _bacc.Bacc("TRN2", target_bir_lowering=False, num_devices=1)
    arrays, aps = {}, {}
    for name, arr in list((n, inputs[n]) for n in NAMES) + list(constants().items()):
        arr = np.ascontiguousarray(arr)
        arrays[f"in_{name}"] = arr
        aps[name] = nc.dram_tensor(f"in_{name}", arr.shape, mybir.dt.from_np(arr.dtype), kind="ExternalInput").ap()
    out = nc.dram_tensor("out_y", (1, T, D), F, kind="ExternalOutput").ap()
    trunk(nc, aps, out)
    r = _run(nc, [arrays], core_ids=[0])
    return r.results[0]["out_y"]
```
